# Optimizing a Trainium2 kernel written in Bass

```python
import math
import jax, jax.numpy as jnp
from jax import lax
import numpy as np
import jax
import jax.numpy as jnp

D_MODEL = 1024
BATCH = 1
SEQ = 256
DEPTH = 2

GRID_W = 64
N_MIXERS = 4
GROUP_WIDTH = D_MODEL // N_MIXERS
HEAD_DIM = 64
Q_BLOCK = 128
EPS = 1e-6

NA_HEADS = GROUP_WIDTH // HEAD_DIM
NA_WIN_ROWS = 8
NA_WIN_COLS = 16

DIFF_HEADS = GROUP_WIDTH // HEAD_DIM
DIFF_QK_DIM = HEAD_DIM // 2
DIFF_V_DIM = HEAD_DIM

GQA_HEADS = GROUP_WIDTH // HEAD_DIM
GQA_KV_HEADS = GQA_HEADS // 2
ROPE_THETA = 10000.0

MLA_HEADS = GROUP_WIDTH // HEAD_DIM
MLA_Q_LORA = GROUP_WIDTH
MLA_KV_LORA = GROUP_WIDTH // 2
MLA_NOPE_DIM = HEAD_DIM
MLA_ROPE_DIM = HEAD_DIM // 2
MLA_V_DIM = HEAD_DIM

D_FF = -(-8 * D_MODEL // (3 * 256)) * 256

IN_SIZES = (
    NA_HEADS * HEAD_DIM, NA_HEADS * HEAD_DIM, NA_HEADS * HEAD_DIM,
    DIFF_HEADS * 2 * DIFF_QK_DIM, DIFF_HEADS * 2 * DIFF_QK_DIM, DIFF_HEADS * DIFF_V_DIM,
    GQA_HEADS * HEAD_DIM, GQA_KV_HEADS * HEAD_DIM, GQA_KV_HEADS * HEAD_DIM,
    MLA_Q_LORA, MLA_KV_LORA, MLA_ROPE_DIM,
)
IN_WIDTH = sum(IN_SIZES)
MIX_WIDTH = NA_HEADS * HEAD_DIM + DIFF_HEADS * DIFF_V_DIM + GQA_HEADS * HEAD_DIM + MLA_HEADS * MLA_V_DIM


def rms_norm(x, w):
    xf = x.astype(jnp.float32)
    y = xf * lax.rsqrt(jnp.mean(xf * xf, axis=-1, keepdims=True) + EPS)
    return (y * w.astype(jnp.float32)).astype(x.dtype)

def rope(x, pos):
    d = x.shape[-1]
    inv = ROPE_THETA ** (-jnp.arange(0, d, 2, dtype=jnp.float32) / d)
    ang = pos.astype(jnp.float32)[:, None] * inv[None, :]
    ang = jnp.concatenate([ang, ang], axis=-1)
    xf = x.astype(jnp.float32)
    x1, x2 = jnp.split(xf, 2, axis=-1)
    rot = jnp.concatenate([-x2, x1], axis=-1)
    return (xf * jnp.cos(ang) + rot * jnp.sin(ang)).astype(x.dtype)

def axial_rope(x, row, col):
    half = x.shape[-1] // 2
    return jnp.concatenate([rope(x[..., :half], row), rope(x[..., half:], col)], axis=-1)

def split_heads(t, n):
    b, s, _ = t.shape
    return t.reshape(b, s, n, -1).transpose(0, 2, 1, 3)

def merge_heads(t):
    b, h, s, d = t.shape
    return t.transpose(0, 2, 1, 3).reshape(b, s, h * d)

def to_blocks(t):
    b, h, s, d = t.shape
    return t.reshape(b, h, s // Q_BLOCK, Q_BLOCK, d).transpose(2, 0, 1, 3, 4)

def from_blocks(t):
    nb, b, h, qb, d = t.shape
    return t.transpose(1, 2, 0, 3, 4).reshape(b, h, nb * qb, d)

def neighbourhood_attention(q, k, v, rel_bias):
    b, h, s, d = q.shape
    rows = s // GRID_W
    wr = min(NA_WIN_ROWS, rows)
    wc = NA_WIN_COLS
    q5 = q.reshape(b, h, rows, GRID_W, d)
    k5 = k.reshape(b, h, rows, GRID_W, d)
    v5 = v.reshape(b, h, rows, GRID_W, d)
    r = jnp.arange(rows)
    row_start = jnp.clip(r - wr // 2, 0, rows - wr)
    c = jnp.arange(GRID_W)
    col_idx = jnp.clip(c - wc // 2, 0, GRID_W - wc)[:, None] + jnp.arange(wc)[None, :]
    dc_idx = col_idx - c[:, None] + (NA_WIN_COLS - 1)
    scale = d ** -0.5

    def row_block(args):
        q_r, rs, r_i = args
        k_band = lax.dynamic_slice_in_dim(k5, rs, wr, axis=2)
        v_band = lax.dynamic_slice_in_dim(v5, rs, wr, axis=2)
        k_win = k_band[:, :, :, col_idx, :]
        v_win = v_band[:, :, :, col_idx, :]
        dr_idx = rs + jnp.arange(wr) - r_i + (NA_WIN_ROWS - 1)
        bias = rel_bias[:, dr_idx[None, :, None], dc_idx[:, None, :]]
        sc = jnp.einsum('bhcd,bhrcwd->bhcrw', q_r, k_win).astype(jnp.float32) * scale + bias.astype(jnp.float32)
        p = jax.nn.softmax(sc.reshape(b, h, GRID_W, wr * wc), axis=-1).reshape(b, h, GRID_W, wr, wc)
        return jnp.einsum('bhcrw,bhrcwd->bhcd', p.astype(v.dtype), v_win)

    out = lax.map(row_block, (q5.transpose(2, 0, 1, 3, 4), row_start, r))
    return out.transpose(1, 2, 0, 3, 4).reshape(b, h, s, d)

def diff_attention(q1, q2, k1, k2, v, lam, slopes):
    s = k1.shape[2]
    pos = jnp.arange(s)
    scale = DIFF_QK_DIM ** -0.5

    def block(args):
        qb1, qb2, qp = args
        dist = jnp.abs(qp[:, None] - pos[None, :]).astype(jnp.float32)
        alibi = -slopes[:, None, None] * dist
        s1 = jnp.einsum('bhqd,bhkd->bhqk', qb1, k1).astype(jnp.float32) * scale + alibi
        s2 = jnp.einsum('bhqd,bhkd->bhqk', qb2, k2).astype(jnp.float32) * scale + alibi
        a = jax.nn.softmax(s1, axis=-1) - lam * jax.nn.softmax(s2, axis=-1)
        return jnp.einsum('bhqk,bhkd->bhqd', a.astype(v.dtype), v)

    out = lax.map(block, (to_blocks(q1), to_blocks(q2), pos.reshape(-1, Q_BLOCK)))
    return from_blocks(out)

def gqa_attention(q, k, v):
    b, h, s, d = q.shape
    kvh = k.shape[1]
    g = h // kvh
    scale = d ** -0.5

    def block(qb):
        qg = qb.reshape(b, kvh, g, Q_BLOCK, d)
        sc = jnp.einsum('bkgqd,bksd->bkgqs', qg, k).astype(jnp.float32) * scale
        o = jnp.einsum('bkgqs,bksd->bkgqd', jax.nn.softmax(sc, axis=-1).astype(v.dtype), v)
        return o.reshape(b, h, Q_BLOCK, d)

    return from_blocks(lax.map(block, to_blocks(q)))

def mla_attention(q_nope, q_rope, k_nope, k_rope, v):
    scale = (MLA_NOPE_DIM + MLA_ROPE_DIM) ** -0.5

    def block(args):
        qn, qr = args
        sc = (jnp.einsum('bhqd,bhkd->bhqk', qn, k_nope)
              + jnp.einsum('bhqd,bkd->bhqk', qr, k_rope)).astype(jnp.float32) * scale
        return jnp.einsum('bhqk,bhkd->bhqd', jax.nn.softmax(sc, axis=-1).astype(v.dtype), v)

    return from_blocks(lax.map(block, (to_blocks(q_nope), to_blocks(q_rope))))

def first_inputs(seed: int = 0) -> dict:
    key = jax.random.key(seed)
    ks = jax.random.split(key, 21)

    def normal(k, shape, scale):
        return scale * jax.random.normal(k, shape, jnp.float32)

    def gain(k, shape):
        return 1.0 + normal(k, shape, 0.05)

    return {
        "x": normal(ks[0], (BATCH, SEQ, D_MODEL), 1.0),
        "pre_mix_norm": gain(ks[1], (DEPTH, D_MODEL)),
        "w_in": normal(ks[2], (DEPTH, D_MODEL, IN_WIDTH), D_MODEL ** -0.5),
        "na_rel_bias": normal(ks[3], (DEPTH, NA_HEADS, 2 * NA_WIN_ROWS - 1, 2 * NA_WIN_COLS - 1), 0.1),
        "diff_lambda_q1": normal(ks[4], (DEPTH, DIFF_QK_DIM), 0.1),
        "diff_lambda_k1": normal(ks[5], (DEPTH, DIFF_QK_DIM), 0.1),
        "diff_lambda_q2": normal(ks[6], (DEPTH, DIFF_QK_DIM), 0.1),
        "diff_lambda_k2": normal(ks[7], (DEPTH, DIFF_QK_DIM), 0.1),
        "diff_subln": gain(ks[8], (DEPTH, DIFF_V_DIM)),
        "gqa_q_norm": gain(ks[9], (DEPTH, HEAD_DIM)),
        "gqa_k_norm": gain(ks[10], (DEPTH, HEAD_DIM)),
        "mla_q_norm": gain(ks[11], (DEPTH, MLA_Q_LORA)),
        "mla_kv_norm": gain(ks[12], (DEPTH, MLA_KV_LORA)),
        "mla_w_uq": normal(ks[13], (DEPTH, MLA_Q_LORA, MLA_HEADS * (MLA_NOPE_DIM + MLA_ROPE_DIM)), MLA_Q_LORA ** -0.5),
        "mla_w_ukv": normal(ks[14], (DEPTH, MLA_KV_LORA, MLA_HEADS * (MLA_NOPE_DIM + MLA_V_DIM)), MLA_KV_LORA ** -0.5),
        "w_o": normal(ks[15], (DEPTH, MIX_WIDTH, D_MODEL), MIX_WIDTH ** -0.5),
        "post_mix_norm": gain(ks[16], (DEPTH, D_MODEL)),
        "pre_ffn_norm": gain(ks[17], (DEPTH, D_MODEL)),
        "ffn_w_gate_up": normal(ks[18], (DEPTH, D_MODEL, 2 * D_FF), D_MODEL ** -0.5),
        "ffn_w_down": normal(ks[19], (DEPTH, D_FF, D_MODEL), D_FF ** -0.5),
        "post_ffn_norm": gain(ks[20], (DEPTH, D_MODEL)),
    }

def first_block(x, pre_mix_norm, w_in, na_rel_bias, diff_lambda_q1, diff_lambda_k1, diff_lambda_q2,
              diff_lambda_k2, diff_subln, gqa_q_norm, gqa_k_norm, mla_q_norm, mla_kv_norm, mla_w_uq,
              mla_w_ukv, w_o, post_mix_norm, pre_ffn_norm, ffn_w_gate_up, ffn_w_down, post_ffn_norm):
    b, s, _ = x.shape
    pos = jnp.arange(s)
    grid_row = pos // GRID_W
    grid_col = pos % GRID_W
    offsets = [int(o) for o in np.cumsum(IN_SIZES)[:-1]]
    alibi_slopes = jnp.asarray([2.0 ** (-8.0 * (i + 1) / DIFF_HEADS) for i in range(DIFF_HEADS)], dtype=jnp.float32)

    for l in range(DEPTH):
        h = rms_norm(x, pre_mix_norm[l])
        proj = jnp.einsum('bsd,de->bse', h, w_in[l])
        (na_q, na_k, na_v, df_q, df_k, df_v, gq_q, gq_k, gq_v,
         ml_cq, ml_ckv, ml_kr) = jnp.split(proj, offsets, axis=-1)

        a_out = neighbourhood_attention(split_heads(na_q, NA_HEADS), split_heads(na_k, NA_HEADS),
                                        split_heads(na_v, NA_HEADS), na_rel_bias[l])

        lambda_init = 0.8 - 0.6 * math.exp(-0.3 * l)
        dq = df_q.reshape(b, s, DIFF_HEADS, 2, DIFF_QK_DIM).transpose(3, 0, 2, 1, 4)
        dk = df_k.reshape(b, s, DIFF_HEADS, 2, DIFF_QK_DIM).transpose(3, 0, 2, 1, 4)
        lam = (jnp.exp(jnp.sum(diff_lambda_q1[l].astype(jnp.float32) * diff_lambda_k1[l].astype(jnp.float32)))
               - jnp.exp(jnp.sum(diff_lambda_q2[l].astype(jnp.float32) * diff_lambda_k2[l].astype(jnp.float32)))
               + lambda_init)
        b_out = diff_attention(dq[0], dq[1], dk[0], dk[1], split_heads(df_v, DIFF_HEADS), lam, alibi_slopes)
        b_out = rms_norm(b_out, diff_subln[l]) * (1.0 - lambda_init)

        cq = axial_rope(rms_norm(split_heads(gq_q, GQA_HEADS), gqa_q_norm[l]), grid_row, grid_col)
        ck = axial_rope(rms_norm(split_heads(gq_k, GQA_KV_HEADS), gqa_k_norm[l]), grid_row, grid_col)
        c_out = gqa_attention(cq, ck, split_heads(gq_v, GQA_KV_HEADS))

        c_q = rms_norm(ml_cq, mla_q_norm[l])
        q_full = split_heads(jnp.einsum('bsr,re->bse', c_q, mla_w_uq[l]), MLA_HEADS)
        q_nope, q_rope = q_full[..., :MLA_NOPE_DIM], rope(q_full[..., MLA_NOPE_DIM:], pos)
        c_kv = rms_norm(ml_ckv, mla_kv_norm[l])
        kv = split_heads(jnp.einsum('bsr,re->bse', c_kv, mla_w_ukv[l]), MLA_HEADS)
        k_nope, mla_v = kv[..., :MLA_NOPE_DIM], kv[..., MLA_NOPE_DIM:]
        k_rope = rope(ml_kr, pos)
        d_out = mla_attention(q_nope, q_rope, k_nope, k_rope, mla_v)

        mix = jnp.concatenate([merge_heads(a_out), merge_heads(b_out),
                               merge_heads(c_out), merge_heads(d_out)], axis=-1)
        mix = jnp.einsum('bse,ed->bsd', mix, w_o[l])
        x = x + rms_norm(mix, post_mix_norm[l])

        h = rms_norm(x, pre_ffn_norm[l])
        gate, up = jnp.split(jnp.einsum('bsd,df->bsf', h, ffn_w_gate_up[l]), 2, axis=-1)
        f = jnp.einsum('bsf,fd->bsd', jax.nn.silu(gate) * up, ffn_w_down[l])
        x = x + rms_norm(f, post_ffn_norm[l])
    return x


N_SLOTS = D_MODEL // HEAD_DIM
A_HEADS = 8
A_LATENT = 128
IDX_HEADS = 8
IDX_DIM = 64
A_TOPK_MAX = 256
B_HEADS = 8
B_KV_HEADS = 2
B_WINDOW = 128
C_HEADS = 16
C_KV_HEADS = 2
CMP_BLOCK = 32
CMP_STRIDE = 16
CMP_HIDDEN = 128
SLC_BLOCK = 64
SLC_COUNT = 8
C_WINDOW = 512
MEM_LEN = 256
X_HEADS = 4
X_HEAD_DIM = 128
D_FF_2 = 2816
N_EXPERTS = 8
TOP_K = 2
D_FF_EXPERT = 3584
REL_BUCKETS = 32
REL_MAX_DIST = 128
SLC_Q_BLOCK = 32
LN_EPS = 1e-5
NEG_INF = -1e30
FORCE_BONUS = 1e6
ALPHA = (2 * DEPTH) ** 0.25
BETA = (8 * DEPTH) ** -0.25
N_EVEN = (DEPTH + 1) // 2
N_ODD = DEPTH // 2
EVEN_WIDTHS = (A_HEADS * HEAD_DIM, A_LATENT, IDX_HEADS * IDX_DIM, IDX_DIM, IDX_HEADS,
               B_HEADS * HEAD_DIM, B_KV_HEADS * HEAD_DIM, B_KV_HEADS * HEAD_DIM)
EVEN_COLS = sum(EVEN_WIDTHS)
ODD_WIDTHS = (C_HEADS * HEAD_DIM,) + (C_KV_HEADS * HEAD_DIM,) * 6 + (3 * C_HEADS,)
ODD_COLS = sum(ODD_WIDTHS)


def split_cols(a, widths):
    cuts = [int(c) for c in np.cumsum(widths)[:-1]]
    return jnp.split(a, cuts, axis=-1)

def layer_norm(x, g, b):
    xf = x.astype(jnp.float32)
    mu = jnp.mean(xf, -1, keepdims=True)
    var = jnp.mean(jnp.square(xf - mu), -1, keepdims=True)
    return ((xf - mu) * lax.rsqrt(var + LN_EPS)).astype(x.dtype) * g + b

def rms_norm_2(x, g):
    xf = x.astype(jnp.float32)
    y = xf * lax.rsqrt(jnp.mean(jnp.square(xf), -1, keepdims=True) + LN_EPS)
    return y.astype(x.dtype) * g

def rel_bucket(dist):
    n = jnp.maximum(dist, 0)
    max_exact = REL_BUCKETS // 2
    nf = jnp.maximum(n, 1).astype(jnp.float32)
    log_b = max_exact + (jnp.log(nf / max_exact) / math.log(REL_MAX_DIST / max_exact)
                         * (REL_BUCKETS - max_exact)).astype(jnp.int32)
    return jnp.where(n < max_exact, n, jnp.minimum(log_b, REL_BUCKETS - 1))

def banded_attention(q, k, v, rel_tbl, window, sinks=None):
    B, S, H, D = q.shape
    kvh = k.shape[2]
    g = H // kvh
    pad = -(-window // Q_BLOCK) * Q_BLOCK
    span = pad + Q_BLOCK
    kp = jnp.pad(k, ((0, 0), (pad, 0), (0, 0), (0, 0)))
    vp = jnp.pad(v, ((0, 0), (pad, 0), (0, 0), (0, 0)))
    dist = np.arange(Q_BLOCK)[:, None] + pad - np.arange(span)[None, :]
    band = jnp.asarray((dist >= 0) & (dist < window))
    bias = rel_tbl.astype(jnp.float32)[rel_bucket(jnp.asarray(dist))]
    bias = bias.transpose(2, 0, 1).reshape(kvh, g, Q_BLOCK, span)
    key_off = jnp.arange(span) - pad

    def block(n):
        t0 = n * Q_BLOCK
        qb = lax.dynamic_slice_in_dim(q, t0, Q_BLOCK, 1).reshape(B, Q_BLOCK, kvh, g, D)
        kb = lax.dynamic_slice_in_dim(kp, t0, span, 1)
        vb = lax.dynamic_slice_in_dim(vp, t0, span, 1)
        logits = jnp.einsum('bqkgd,bskd->bkgqs', qb, kb).astype(jnp.float32) * D ** -0.5 + bias
        ok = band & (t0 + key_off >= 0)[None, :]
        logits = jnp.where(ok, logits, NEG_INF)
        if sinks is None:
            p = jax.nn.softmax(logits, axis=-1)
        else:
            s = sinks.astype(jnp.float32).reshape(kvh, g, 1, 1)
            m = jnp.maximum(jnp.max(logits, -1, keepdims=True), s)
            e = jnp.exp(logits - m)
            p = e / (jnp.sum(e, -1, keepdims=True) + jnp.exp(s - m))
        o = jnp.einsum('bkgqs,bskd->bqkgd', p.astype(v.dtype), vb)
        return o.reshape(B, Q_BLOCK, H, D)

    out = lax.map(block, jnp.arange(S // Q_BLOCK))
    return jnp.moveaxis(out, 0, 1).reshape(B, S, H, D)

def dsa_attention(q_a, c_kv, q_i, k_i, w_i, ckv_gain, w_uk, w_uv, rel_tbl):
    B, S, _ = q_a.shape
    topk = min(A_TOPK_MAX, S // 4)
    q_lat = jnp.einsum('bshd,hdc->bshc', q_a.reshape(B, S, A_HEADS, HEAD_DIM), w_uk)
    c = rms_norm_2(c_kv, ckv_gain)
    qi = q_i.reshape(B, S, IDX_HEADS, IDX_DIM)
    wi = w_i * IDX_HEADS ** -0.5
    tbl = rel_tbl.astype(jnp.float32)
    kpos = jnp.arange(S)

    def block(n):
        t0 = n * Q_BLOCK
        qpos = t0 + jnp.arange(Q_BLOCK)
        qi_b = lax.dynamic_slice_in_dim(qi, t0, Q_BLOCK, 1)
        wi_b = lax.dynamic_slice_in_dim(wi, t0, Q_BLOCK, 1)
        ql_b = lax.dynamic_slice_in_dim(q_lat, t0, Q_BLOCK, 1)
        act = jax.nn.relu(jnp.einsum('bqhd,bsd->bqhs', qi_b, k_i) * IDX_DIM ** -0.5)
        score = jnp.einsum('bqh,bqhs->bqs', wi_b, act).astype(jnp.float32)
        score = jnp.where(kpos[None, :] <= qpos[:, None], score, NEG_INF)
        _, sel = lax.top_k(score, topk)
        c_sel = jax.vmap(lambda cb, sb: cb[sb])(c, sel)
        dist = qpos[None, :, None] - sel
        bias = tbl[rel_bucket(dist)].transpose(0, 1, 3, 2)
        lg = jnp.einsum('bqhc,bqkc->bqhk', ql_b, c_sel).astype(jnp.float32) * HEAD_DIM ** -0.5 + bias
        lg = jnp.where((dist >= 0)[:, :, None, :], lg, NEG_INF)
        p = jax.nn.softmax(lg, axis=-1).astype(c.dtype)
        o_lat = jnp.einsum('bqhk,bqkc->bqhc', p, c_sel)
        return jnp.einsum('bqhc,hcd->bqhd', o_lat, w_uv)

    out = lax.map(block, jnp.arange(S // Q_BLOCK))
    return jnp.moveaxis(out, 0, 1).reshape(B, S, A_HEADS, HEAD_DIM)

def compress_blocks(kv, pe, w1, w2):
    B, S, G, D = kv.shape
    n_cmp = (S - CMP_BLOCK) // CMP_STRIDE + 1
    idx = np.arange(n_cmp)[:, None] * CMP_STRIDE + np.arange(CMP_BLOCK)[None, :]
    blk = kv[:, idx] + pe[None, None, :, None, :]
    blk = blk.transpose(0, 1, 3, 2, 4).reshape(B, n_cmp, G, CMP_BLOCK * D)
    return jax.nn.gelu(blk @ w1) @ w2

def nsa_attention(q, k_cmp, v_cmp, k_slc, v_slc, k_win, v_win, gate_logits,
                  pe_k, w1_k, w2_k, pe_v, w1_v, w2_v, rel_tbl):
    B, S, H, D = q.shape
    G = C_KV_HEADS
    hpg = H // G
    qg = q.reshape(B, S, G, hpg, D)
    scale = D ** -0.5
    tbl = rel_tbl.astype(jnp.float32)
    pos = np.arange(S)

    n_cmp = (S - CMP_BLOCK) // CMP_STRIDE + 1
    kc = compress_blocks(k_cmp, pe_k, w1_k, w2_k)
    vc = compress_blocks(v_cmp, pe_v, w1_v, w2_v)
    cmp_end = np.arange(n_cmp) * CMP_STRIDE + CMP_BLOCK - 1
    dist_c = pos[:, None] - cmp_end[None, :]
    valid_c = jnp.asarray(dist_c >= 0)
    bias_c = tbl[rel_bucket(jnp.asarray(dist_c))].transpose(2, 0, 1).reshape(G, hpg, S, n_cmp)
    lg = jnp.einsum('bsghd,bngd->bghsn', qg, kc).astype(jnp.float32) * scale + bias_c
    p_cmp = jax.nn.softmax(jnp.where(valid_c, lg, NEG_INF), axis=-1) * valid_c
    o_cmp = jnp.einsum('bghsn,bngd->bsghd', p_cmp.astype(vc.dtype), vc).reshape(B, S, H, D)

    n_slc = S // SLC_BLOCK
    n_sel = min(SLC_COUNT, n_slc)
    cs = np.arange(n_cmp)[:, None] * CMP_STRIDE
    ss = np.arange(n_slc)[None, :] * SLC_BLOCK
    overlap = jnp.asarray(((cs < ss + SLC_BLOCK) & (cs + CMP_BLOCK > ss)).astype(np.float32))
    p_slc = jnp.einsum('bghsn,nj->bgsj', p_cmp, overlap)
    blk = pos // SLC_BLOCK
    jj = np.arange(n_slc)
    forced = (jj[None, :] == 0) | (jj[None, :] == blk[:, None]) | (jj[None, :] == blk[:, None] - 1)
    admissible = jj[None, :] * SLC_BLOCK <= pos[:, None]
    score = jnp.where(jnp.asarray(admissible),
                      p_slc + FORCE_BONUS * jnp.asarray(forced.astype(np.float32)), NEG_INF)
    _, sel = lax.top_k(score, n_sel)

    kb = k_slc.reshape(B, n_slc, SLC_BLOCK, G, D).transpose(0, 3, 1, 2, 4)
    vb = v_slc.reshape(B, n_slc, SLC_BLOCK, G, D).transpose(0, 3, 1, 2, 4)
    bi = jnp.arange(B)[:, None, None, None]
    gi = jnp.arange(G)[None, :, None, None]
    tbl_g = tbl.reshape(REL_BUCKETS, G, hpg).transpose(1, 0, 2)
    in_blk = jnp.arange(SLC_BLOCK)
    n_keys = n_sel * SLC_BLOCK

    def slc_block(n):
        t0 = n * SLC_Q_BLOCK
        qpos = t0 + jnp.arange(SLC_Q_BLOCK)
        qb = lax.dynamic_slice_in_dim(qg, t0, SLC_Q_BLOCK, 1)
        sb = lax.dynamic_slice_in_dim(sel, t0, SLC_Q_BLOCK, 2)
        ks = kb[bi, gi, sb].reshape(B, G, SLC_Q_BLOCK, n_keys, D)
        vs = vb[bi, gi, sb].reshape(B, G, SLC_Q_BLOCK, n_keys, D)
        kpos = (sb[..., None] * SLC_BLOCK + in_blk).reshape(B, G, SLC_Q_BLOCK, n_keys)
        dist = qpos[None, None, :, None] - kpos
        bias = tbl_g[gi, rel_bucket(dist)].transpose(0, 1, 4, 2, 3)
        lg2 = jnp.einsum('bqghd,bgqsd->bghqs', qb, ks).astype(jnp.float32) * scale + bias
        lg2 = jnp.where((dist >= 0)[:, :, None], lg2, NEG_INF)
        p = jax.nn.softmax(lg2, axis=-1).astype(vs.dtype)
        o = jnp.einsum('bghqs,bgqsd->bqghd', p, vs)
        return o.reshape(B, SLC_Q_BLOCK, H, D)

    o_slc = lax.map(slc_block, jnp.arange(S // SLC_Q_BLOCK))
    o_slc = jnp.moveaxis(o_slc, 0, 1).reshape(B, S, H, D)

    o_win = banded_attention(q, k_win, v_win, rel_tbl, C_WINDOW)

    gt = jax.nn.sigmoid(gate_logits).reshape(B, S, H, 3)
    return gt[..., 0:1] * o_cmp + gt[..., 1:2] * o_slc + gt[..., 2:3] * o_win

def even_mixer(x, w_in, ckv_gain, w_uk, w_uv, sinks, w_out, rel_table):
    B, S, _ = x.shape
    q_a, c_kv, q_i, k_i, w_i, q_b, k_b, v_b = split_cols(x @ w_in, EVEN_WIDTHS)
    o_a = dsa_attention(q_a, c_kv, q_i, k_i, w_i, ckv_gain, w_uk, w_uv, rel_table[:, :A_HEADS])
    o_b = banded_attention(q_b.reshape(B, S, B_HEADS, HEAD_DIM),
                           k_b.reshape(B, S, B_KV_HEADS, HEAD_DIM),
                           v_b.reshape(B, S, B_KV_HEADS, HEAD_DIM),
                           rel_table[:, A_HEADS:A_HEADS + B_HEADS], B_WINDOW, sinks)
    o = jnp.concatenate([o_a.reshape(B, S, -1), o_b.reshape(B, S, -1)], axis=-1)
    return o @ w_out

def odd_mixer(x, w_in, pe_k, w1_k, w2_k, pe_v, w1_v, w2_v, w_out, rel_table):
    B, S, _ = x.shape
    q, kc, vc, ks, vs, kw, vw, gl = split_cols(x @ w_in, ODD_WIDTHS)
    r = lambda a, h: a.reshape(B, S, h, HEAD_DIM)
    o = nsa_attention(r(q, C_HEADS), r(kc, C_KV_HEADS), r(vc, C_KV_HEADS), r(ks, C_KV_HEADS),
                      r(vs, C_KV_HEADS), r(kw, C_KV_HEADS), r(vw, C_KV_HEADS), gl,
                      pe_k, w1_k, w2_k, pe_v, w1_v, w2_v, rel_table[:, :C_HEADS])
    return o.reshape(B, S, C_HEADS * HEAD_DIM) @ w_out

def cross_attention(x, mem, w_q, w_k, w_v, w_o):
    B, S, _ = x.shape
    M = mem.shape[1]
    q = (x @ w_q).reshape(B, S, X_HEADS, X_HEAD_DIM)
    k = (mem @ w_k).reshape(B, M, X_HEADS, X_HEAD_DIM)
    v = (mem @ w_v).reshape(B, M, X_HEADS, X_HEAD_DIM)
    lg = jnp.einsum('bshd,bmhd->bhsm', q, k).astype(jnp.float32) * X_HEAD_DIM ** -0.5
    p = jax.nn.softmax(lg, axis=-1).astype(v.dtype)
    o = jnp.einsum('bhsm,bmhd->bshd', p, v).reshape(B, S, X_HEADS * X_HEAD_DIM)
    return o @ w_o

def dense_swiglu(x, w_gate, w_up, w_down):
    return (jax.nn.silu(x @ w_gate) * (x @ w_up)) @ w_down

def moe_swiglu(x, w_router, w_gate, w_up, w_down):
    logits = (x @ w_router).astype(jnp.float32)
    top_val, top_idx = lax.top_k(logits, TOP_K)
    top_w = jax.nn.softmax(top_val, axis=-1)
    gate = jnp.einsum('bsk,bske->bse', top_w,
                      jax.nn.one_hot(top_idx, N_EXPERTS, dtype=jnp.float32)).astype(x.dtype)
    y = jnp.zeros_like(x)
    for e in range(N_EXPERTS):
        h = jax.nn.silu(x @ w_gate[e]) * (x @ w_up[e])
        y = y + gate[..., e:e + 1] * (h @ w_down[e])
    return y

def second_inputs(seed: int = 0) -> dict:
    key = jax.random.key(seed)
    ks = iter(jax.random.split(key, 32))

    def nrm(shape, scale):
        return jax.random.normal(next(ks), shape, jnp.float32) * scale

    D = D_MODEL
    XW = X_HEADS * X_HEAD_DIM
    CW = CMP_BLOCK * HEAD_DIM
    return {
        'x': nrm((BATCH, SEQ, D), 1.0),
        'mem': nrm((BATCH, MEM_LEN, D), 1.0),
        'rel_table': nrm((REL_BUCKETS, N_SLOTS), 0.2),
        'ev_w_in': nrm((N_EVEN, D, EVEN_COLS), D ** -0.5),
        'ev_ckv_gain': 1.0 + nrm((N_EVEN, A_LATENT), 0.02),
        'ev_w_uk': nrm((N_EVEN, A_HEADS, HEAD_DIM, A_LATENT), HEAD_DIM ** -0.5),
        'ev_w_uv': nrm((N_EVEN, A_HEADS, A_LATENT, HEAD_DIM), A_LATENT ** -0.5),
        'ev_sinks': nrm((N_EVEN, B_HEADS), 0.5),
        'ev_w_out': nrm((N_EVEN, N_SLOTS * HEAD_DIM, D), BETA * (N_SLOTS * HEAD_DIM) ** -0.5),
        'od_w_in': nrm((N_ODD, D, ODD_COLS), D ** -0.5),
        'od_pe_k': nrm((N_ODD, CMP_BLOCK, HEAD_DIM), 0.1),
        'od_w1_k': nrm((N_ODD, CW, CMP_HIDDEN), CW ** -0.5),
        'od_w2_k': nrm((N_ODD, CMP_HIDDEN, HEAD_DIM), CMP_HIDDEN ** -0.5),
        'od_pe_v': nrm((N_ODD, CMP_BLOCK, HEAD_DIM), 0.1),
        'od_w1_v': nrm((N_ODD, CW, CMP_HIDDEN), CW ** -0.5),
        'od_w2_v': nrm((N_ODD, CMP_HIDDEN, HEAD_DIM), CMP_HIDDEN ** -0.5),
        'od_w_out': nrm((N_ODD, C_HEADS * HEAD_DIM, D), BETA * (C_HEADS * HEAD_DIM) ** -0.5),
        'xa_w_q': nrm((DEPTH, D, XW), D ** -0.5),
        'xa_w_k': nrm((DEPTH, D, XW), D ** -0.5),
        'xa_w_v': nrm((DEPTH, D, XW), D ** -0.5),
        'xa_w_o': nrm((DEPTH, XW, D), BETA * XW ** -0.5),
        'ff_w_gate': nrm((N_EVEN, D, D_FF_2), D ** -0.5),
        'ff_w_up': nrm((N_EVEN, D, D_FF_2), D ** -0.5),
        'ff_w_down': nrm((N_EVEN, D_FF_2, D), BETA * D_FF_2 ** -0.5),
        'moe_w_router': nrm((N_ODD, D, N_EXPERTS), D ** -0.5),
        'moe_w_gate': nrm((N_ODD, N_EXPERTS, D, D_FF_EXPERT), D ** -0.5),
        'moe_w_up': nrm((N_ODD, N_EXPERTS, D, D_FF_EXPERT), D ** -0.5),
        'moe_w_down': nrm((N_ODD, N_EXPERTS, D_FF_EXPERT, D), BETA * D_FF_EXPERT ** -0.5),
        'ln_g': 1.0 + nrm((DEPTH, 3, D), 0.02),
        'ln_b': nrm((DEPTH, 3, D), 0.02),
    }

def second_block(x, mem, rel_table, ev_w_in, ev_ckv_gain, ev_w_uk, ev_w_uv, ev_sinks, ev_w_out,
              od_w_in, od_pe_k, od_w1_k, od_w2_k, od_pe_v, od_w1_v, od_w2_v, od_w_out,
              xa_w_q, xa_w_k, xa_w_v, xa_w_o, ff_w_gate, ff_w_up, ff_w_down,
              moe_w_router, moe_w_gate, moe_w_up, moe_w_down, ln_g, ln_b):
    h = x
    for i in range(DEPTH):
        j = i // 2
        if i % 2 == 0:
            mix = even_mixer(h, ev_w_in[j], ev_ckv_gain[j], ev_w_uk[j], ev_w_uv[j], ev_sinks[j],
                             ev_w_out[j], rel_table)
        else:
            mix = odd_mixer(h, od_w_in[j], od_pe_k[j], od_w1_k[j], od_w2_k[j], od_pe_v[j],
                            od_w1_v[j], od_w2_v[j], od_w_out[j], rel_table)
        h = layer_norm(ALPHA * h + mix, ln_g[i, 0], ln_b[i, 0])
        xa = cross_attention(h, mem, xa_w_q[i], xa_w_k[i], xa_w_v[i], xa_w_o[i])
        h = layer_norm(ALPHA * h + xa, ln_g[i, 1], ln_b[i, 1])
        if i % 2 == 0:
            ff = dense_swiglu(h, ff_w_gate[j], ff_w_up[j], ff_w_down[j])
        else:
            ff = moe_swiglu(h, moe_w_router[j], moe_w_gate[j], moe_w_up[j], moe_w_down[j])
        h = layer_norm(ALPHA * h + ff, ln_g[i, 2], ln_b[i, 2])
    return h


def setup_inputs(seed=0):
    out = dict(first_inputs(seed))
    for name, value in second_inputs(seed + 1).items():
        if name != "x":
            out[name + "_2"] = value
    return out


def reference(
    x, pre_mix_norm, w_in, na_rel_bias, diff_lambda_q1, diff_lambda_k1, diff_lambda_q2,
    diff_lambda_k2, diff_subln, gqa_q_norm, gqa_k_norm, mla_q_norm, mla_kv_norm, mla_w_uq,
    mla_w_ukv, w_o, post_mix_norm, pre_ffn_norm, ffn_w_gate_up, ffn_w_down, post_ffn_norm,
    mem_2, rel_table_2, ev_w_in_2, ev_ckv_gain_2, ev_w_uk_2, ev_w_uv_2, ev_sinks_2, ev_w_out_2,
    od_w_in_2, od_pe_k_2, od_w1_k_2, od_w2_k_2, od_pe_v_2, od_w1_v_2, od_w2_v_2, od_w_out_2,
    xa_w_q_2, xa_w_k_2, xa_w_v_2, xa_w_o_2, ff_w_gate_2, ff_w_up_2, ff_w_down_2, moe_w_router_2,
    moe_w_gate_2, moe_w_up_2, moe_w_down_2, ln_g_2, ln_b_2,
):
    x = first_block(
        x, pre_mix_norm, w_in, na_rel_bias, diff_lambda_q1, diff_lambda_k1, diff_lambda_q2,
        diff_lambda_k2, diff_subln, gqa_q_norm, gqa_k_norm, mla_q_norm, mla_kv_norm, mla_w_uq,
        mla_w_ukv, w_o, post_mix_norm, pre_ffn_norm, ffn_w_gate_up, ffn_w_down, post_ffn_norm,
    )
    return second_block(
        x, mem_2, rel_table_2, ev_w_in_2, ev_ckv_gain_2, ev_w_uk_2, ev_w_uv_2, ev_sinks_2,
        ev_w_out_2, od_w_in_2, od_pe_k_2, od_w1_k_2, od_w2_k_2, od_pe_v_2, od_w1_v_2, od_w2_v_2,
        od_w_out_2, xa_w_q_2, xa_w_k_2, xa_w_v_2, xa_w_o_2, ff_w_gate_2, ff_w_up_2, ff_w_down_2,
        moe_w_router_2, moe_w_gate_2, moe_w_up_2, moe_w_down_2, ln_g_2, ln_b_2,
    )


_drawn_inputs = setup_inputs


def setup_inputs(seed=0):
    import zlib

    import numpy as np

    out = dict(_drawn_inputs(seed))
    spreads = {}
    factors = {'gqa_q_norm': 4.39,
     'gqa_k_norm': 4.736,
     'mla_q_norm': 3.702,
     'ev_ckv_gain_2': 8.0,
     'ev_sinks_2': 64.0,
     'od_pe_k_2': 22.618,
     'od_pe_v_2': 4.062}
    for name, (base, spread) in spreads.items():
        noise = np.random.default_rng([zlib.crc32(name.encode()), seed]).standard_normal(out[name].shape)
        drawn = base * np.exp(spread * noise) if base else spread * noise
        out[name] = jnp.asarray(drawn.astype(out[name].dtype))
    for name, factor in factors.items():
        out[name] = (out[name] * factor).astype(out[name].dtype)
    return out
```

```python
import math
from contextlib import ExitStack, contextmanager

import numpy as np

import concourse.bass as bass
from concourse import mybir

F32 = mybir.dt.float32
U32 = mybir.dt.uint32
ALU = mybir.AluOpType
ACT = mybir.ActivationFunctionType
AX = mybir.AxisListType.X

P = 128
D = 1024
S = 256
T = S // P
KD = D // P
DEPTH = 2
GRID_W = 64
ROWS = S // GRID_W
NA_ROWS, NA_COLS = 8, 16
HD = 64
EPS, LN_EPS = 1e-6, 1e-5
ALPHA = (2 * DEPTH) ** 0.25
NEG = -1e30
IN_W = 2464
EV_W = 1992
OD_W = 1840
D_FF = 2816
D_EXP = 3584
EXPERTS = 8
TOPK = 64
CMP = 15
SLOT = 4096
SLOTS = 6
RINGS = {"a": 2, "d": 2, "x": 4}
BODY = 2
BIAS_SLOTS = 3
VEC_SLOTS = 3
NEAR = 2 * ROWS - 1
ROPE_THETA = 10000.0

NA_Q, NA_K, NA_V, DF_Q, DF_K, DF_V = 0, 256, 512, 768, 1024, 1280
GQ_Q, GQ_K, GQ_V, ML_Q, ML_KV, ML_KR = 1536, 1792, 1920, 2048, 2304, 2432
SV_GQ, SV_GK, SV_MQ, SV_MKV, SV_SUB, SV_LAM, SV_END = 0, 64, 128, 384, 512, 576, 704


def shape_constants():
    f = np.float32
    pos = np.arange(S)
    inv = (f(ROPE_THETA) ** (-np.arange(0, 32, 2, dtype=f) / f(32))).astype(f)
    rope = np.zeros((S, 3, 2, 16), f)
    for n, where in enumerate((pos // GRID_W, pos % GRID_W, pos)):
        angle = (where.astype(f)[:, None] * inv[None, :]).astype(f)
        rope[:, n, 0], rope[:, n, 1] = np.cos(angle), np.sin(angle)
    c = np.arange(GRID_W)
    start = np.clip(c - NA_COLS // 2, 0, GRID_W - NA_COLS)
    window = np.where((c[None] >= start[:, None]) & (c[None] < start[:, None] + NA_COLS), f(0), f(NEG))
    window = np.tile(window, (P // GRID_W, ROWS)).astype(f)
    dist = 255 - np.arange(512)
    apart = pos[:, None] - pos[None]
    alibi = np.stack([-f(2.0 ** (-8.0 * (h + 1) / 4)) * np.abs(apart).astype(f) for h in range(4)])
    after = np.where(apart >= 0, f(0), f(NEG))
    n = np.maximum(dist, 0)
    nf = np.maximum(n, 1).astype(f)
    log_b = 16 + (np.log(nf / f(16)) / f(math.log(8)) * f(16)).astype(np.int32)
    bucket = np.where(n < 16, n, np.minimum(log_b, 31))
    onehot = (np.arange(32)[:, None] == bucket[None]).astype(f)
    causal = np.where(dist >= 0, f(0), f(NEG))
    band = np.where((dist >= 0) & (dist < 128), f(0), f(NEG))
    return {
        "c_ident": np.eye(P, dtype=f), "c_rope": rope, "c_window": window, "c_alibi": alibi.astype(f),
        "c_bucket": onehot, "c_line": np.stack([causal, band]).astype(f),
        "c_index": np.arange(8, dtype=f)[None],
        "c_causal": after.astype(f),
    }


class Lane:

    def __init__(self, book, name, landed):
        self.book, self.name, self.landed = book, name, landed
        self.count, self.last = {}, None
        self.turn = None
        self.ring = {r: 0 for r in RINGS}

    def tick(self, sem, *keys, by=1):
        self.count[sem.name] = self.count.get(sem.name, 0) + by
        self.last = (sem, self.count[sem.name])
        self.mark(*keys)
        return sem, by

    def mark(self, *keys):
        if self.last:
            for key in keys:
                self.book["new"][key] = (*self.last, self.turn is not None)

    def of(self, key, before=False):
        known = self.book["known"].get(key)
        if known is None:
            assert self.book["first"] or key[0] == "done", key
            return self.landed, 16
        name, value, looped = known[0].name, known[1], known[2]
        sem = self.book["sems"][name]
        step = self.book["step"].get(name, 0)
        if self.turn is not None and looped:
            value = value - (step if before else 0)
            assert value > 0, key
            return sem, self.turn * step + value
        return sem, value + (step * (self.book["turns"] - 1) if looped else 0)

    def own(self):
        sem, value = self.last or (self.landed, 16)
        if self.turn is not None:
            return sem, self.turn * self.book["step"].get(sem.name, 0) + value
        return sem, value

    def back(self, what, n, first=0, body=0):
        if n < 0:
            return self.landed, 16
        if self.turn is not None and n < first:
            return self.of((*what, n + body), before=True)
        return self.of((*what, n))

    @contextmanager
    def loop(self, eng, turns):
        start = dict(self.count)
        with eng.Fori(0, turns) as turn:
            self.turn = turn
            yield turn
            self.turn = None
        for name, value in self.count.items():
            step = value - start.get(name, 0)
            if step:
                self.book["step_new"][name] = step
                self.count[name] = value + step * (turns - 1)
        self.last = (self.last[0], self.count[self.last[0].name])


def plan(a):
    stages, blocks, biases, vectors = [], [], [], []

    def block(src, p, k, c):
        blocks.append((src, p, k, c))
        return len(blocks) - 1

    def columns(w, width, k=KD):
        view = w.rearrange("(k p) c -> p k c", p=P)
        out = []
        for c0 in range(0, width, 512):
            c = min(512, width - c0)
            out.append((block(view[:, :, c0:c0 + c], P, k, c), c0, c))
        return out

    def vector(src):
        vectors.append(src)
        return len(vectors) - 1

    def bias(*what):
        biases.append(what)
        return len(biases) - 1

    def stage(kind, **args):
        stages.append((kind, args))

    def ffn(gate, up, down, width):
        gv, uv = (w.rearrange("(k p) c -> p k c", p=P) for w in (gate, up))
        widths = [min(512, width - c0) for c0 in range(0, width, 512)]
        groups, late = [], None
        for g, w in enumerate(widths):
            c0 = 512 * g
            gb = block(gv[:, :, c0:c0 + w], P, KD, w)
            ub = block(uv[:, :, c0:c0 + w], P, KD, w)
            if late is not None:
                groups[-1]["down"] = block(late, P, groups[-1]["w"] // P, D)
            late = down[c0:c0 + w, :].rearrange("(k p) c -> p k c", p=P)
            groups.append({"gate": gb, "up": ub, "w": w})
        groups[-1]["down"] = block(late, P, widths[-1] // P, D)
        return groups

    stage("load_x")
    stage("lines")
    for l in range(DEPTH):
        stage("small", l=l)
        stage("rms_pre", vec=vector(a["pre_mix_norm"][l]))
        stage("turn", src="N", dst="hT", chunks=KD)
        stage("linear", lhs="hT", k=KD, blocks=columns(a["w_in"][l], IN_W), dst="proj")
        stage("head_norms", l=l)
        stage("turn", src="mla_lat", dst="hT", chunks=3)
        uq = block(a["mla_w_uq"][l].rearrange("(k p) c -> p k c", p=P), P, 2, 384)
        ukv = block(a["mla_w_ukv"][l].rearrange("(k p) c -> p k c", p=P), P, 1, 512)
        stage("linear", lhs="hT", k=2, blocks=[(uq, 0, 384)], dst="QF")
        stage("linear", lhs="hT2", k=1, blocks=[(ukv, 0, 512)], dst="KV")
        stage("mla_keys", l=l)
        jobs = []
        for h in range(4):
            jobs.append(dict(q=("proj", NA_Q + HD * h), k=("proj", NA_K + HD * h), v=("proj", NA_V + HD * h), d=HD,
                             dv=HD, scale=HD ** -0.5, bias=bias("na", l, h), out=("O", HD * h)))
        for h in range(4):
            b = bias("alibi", h)
            for j in range(2):
                o = 64 * h + 32 * j
                jobs.append(dict(q=("proj", DF_Q + o), k=("proj", DF_K + o), v=("proj", DF_V + HD * h), d=32,
                                 dv=HD, scale=32 ** -0.5, bias=b, out=("DO", 256 * j + HD * h)))
        for h in range(4):
            jobs.append(dict(q=("proj", GQ_Q + HD * h), k=("proj", GQ_K + HD * (h // 2)),
                             v=("proj", GQ_V + HD * (h // 2)), d=HD, dv=HD, scale=HD ** -0.5, bias=None,
                             out=("O", 512 + HD * h)))
        for h in range(4):
            jobs.append(dict(q=("QF", 96 * h), k=("KF", 96 * h), v=("KV", 128 * h + 64), d=96, dv=HD,
                             scale=96 ** -0.5, bias=None, out=("O", 768 + HD * h)))
        stage("attend", jobs=jobs)
        stage("diff_out", l=l)
        stage("turn", src="O", dst="hT", chunks=KD)
        stage("linear", lhs="hT", k=KD, blocks=columns(a["w_o"][l], D), dst="N")
        stage("rms_add", vec=vector(a["post_mix_norm"][l]))
        stage("rms_pre", vec=vector(a["pre_ffn_norm"][l]))
        stage("turn", src="N", dst="hT", chunks=KD)
        gu = a["ffn_w_gate_up"][l]
        stage("ffn", groups=ffn(gu[:, 0:D_FF], gu[:, D_FF:2 * D_FF], a["ffn_w_down"][l], D_FF))
        stage("rms_add", vec=vector(a["post_ffn_norm"][l]))

    def cross(i):
        stage("turn", src="X", dst="hT", chunks=KD)
        stage("linear", lhs="hT", k=KD, blocks=columns(a["xa_w_q_2"][i], 512), dst="proj")
        stage("linear", lhs="memT", k=KD, blocks=columns(a["xa_w_k_2"][i], 512), dst="proj@512")
        stage("linear", lhs="memT", k=KD, blocks=columns(a["xa_w_v_2"][i], 512), dst="proj@1024")
        stage("attend", jobs=[dict(q=("proj", P * h), k=("proj", 512 + P * h), v=("proj", 1024 + P * h), d=P, dv=P,
                                   scale=P ** -0.5, bias=None, out=("O", P * h)) for h in range(4)])
        stage("turn", src="O", dst="hT", chunks=4)
        wo = block(a["xa_w_o_2"][i].rearrange("(k p) c -> p k c", p=P), P, 4, D)
        stage("linear", lhs="hT", k=4, blocks=[(wo, 0, D)], dst="N")
        norm(i, 1)

    def norm(i, j):
        stage("layer_norm", gain=vector(a["ln_g_2"][i, j]), shift=vector(a["ln_b_2"][i, j]))

    stage("load_mem")
    stage("turn", src="N", dst="memT", chunks=KD)
    stage("turn", src="X", dst="hT", chunks=KD)
    stage("linear", lhs="hT", k=KD, blocks=columns(a["ev_w_in_2"][0], EV_W), dst="proj")
    stage("latent_norm")
    stage("index_scores")
    stage("select", bias=bias("line", "causal"))
    uk = block(a["ev_w_uk_2"][0].rearrange("h d c -> d h c"), HD, 8, P)
    uv = block(a["ev_w_uv_2"][0].rearrange("h c d -> c h d"), P, 8, HD)
    stage("latent_heads", uk=uk, uv=uv)
    jobs = []
    for h in range(8):
        g = h // 4
        jobs.append(dict(q=("proj", 1224 + HD * h), k=("proj", 1736 + HD * g), v=("proj", 1864 + HD * g), d=HD, dv=HD,
                         scale=HD ** -0.5, bias=bias("band", h + 8), sink=h, out=("O", 512 + HD * h)))
    for h in range(8):
        jobs.append(dict(qT=("QL", h), kT="cT", v=("VC", HD * h), d=P, dv=HD, scale=HD ** -0.5,
                         bias=bias("causal", h), selected=True, out=("O", HD * h)))
    stage("attend", jobs=jobs)
    stage("turn", src="O", dst="hT", chunks=KD)
    stage("linear", lhs="hT", k=KD, blocks=columns(a["ev_w_out_2"][0], D), dst="N")
    norm(0, 0)
    cross(0)
    stage("turn", src="X", dst="hT", chunks=KD)
    stage("ffn", groups=ffn(a["ff_w_gate_2"][0], a["ff_w_up_2"][0], a["ff_w_down_2"][0], D_FF))
    norm(0, 2)
    stage("turn", src="X", dst="hT", chunks=KD)
    stage("linear", lhs="hT", k=KD, blocks=columns(a["od_w_in_2"][0], OD_W), dst="proj")
    stage("gates")
    for n, x in enumerate("kv"):
        w1 = block(a[f"od_w1_{x}_2"][0].rearrange("(i d) c -> d i c", d=HD), HD, 32, P)
        w2 = block(a[f"od_w2_{x}_2"][0].rearrange("(k p) c -> p k c", p=P), P, 1, HD)
        stage("compress", n=n, w1=w1, w2=w2)
    jobs = []
    for h in range(16):
        g = h // 8
        b = bias("causal", h)
        q = ("proj", HD * h)
        common = dict(q=q, d=HD, dv=HD, scale=HD ** -0.5, bias=b, out=("O", HD * h))
        jobs.append(dict(common, kT=("KC", g), v=("VCMP", g), keys=CMP, gate=3 * h))
        jobs.append(dict(common, k=("proj", 1280 + HD * g), v=("proj", 1408 + HD * g), gate=3 * h + 1, add=True))
        jobs.append(dict(common, k=("proj", 1536 + HD * g), v=("proj", 1664 + HD * g), gate=3 * h + 2, add=True))
    stage("attend", jobs=jobs)
    stage("turn", src="O", dst="hT", chunks=KD)
    stage("linear", lhs="hT", k=KD, blocks=columns(a["od_w_out_2"][0], D), dst="N")
    norm(1, 0)
    cross(1)
    stage("turn", src="X", dst="hT", chunks=KD)
    stage("linear", lhs="hT", k=KD, blocks=columns(a["moe_w_router_2"][0], EXPERTS), dst="logits")
    stage("route")
    first = len(blocks)
    groups = [ffn(a["moe_w_gate_2"][0, u], a["moe_w_up_2"][0, u], a["moe_w_down_2"][0, u], D_EXP)
              for u in range(BODY)]
    stage("experts", groups=groups, first=first, body=len(blocks) - first)
    norm(1, 2)
    stage("store_x")
    for kind, args in stages:
        if kind == "attend":
            last = {}
            for n, j in enumerate(args["jobs"]):
                last[j["bias"]] = n
            for n, j in enumerate(args["jobs"]):
                j["bias_last"] = last[j["bias"]] == n
    return stages, blocks, biases, vectors


def build(nc, a, out, book, cut=None):
    stages, blocks, biases, vectors = plan(a)
    if cut is not None:
        stages = stages[:cut] + [("store_x", {})]
    expert_stage = [s for s in stages if s[0] == "experts"]
    loop_first = expert_stage[0][1]["first"] if expert_stage else None
    used_blocks = {b[0] for _, s in stages for b in s.get("blocks", [])}
    for _, s in stages:
        for g in s.get("groups", []):
            for x in (g if isinstance(g, list) else [g]):
                used_blocks |= {x["gate"], x["up"], x["down"]}
        used_blocks |= {s[k] for k in ("uk", "uv", "w1", "w2") if k in s}
    blocks = blocks[:max(used_blocks | {-1}) + 1]
    used_bias = {s["bias"] for _, s in stages if "bias" in s} | {j["bias"] for _, s in stages for j in s.get("jobs", [])}
    biases = biases[:max([b for b in used_bias if b is not None], default=-1) + 1]
    vectors = vectors[:max([s[k] for _, s in stages for k in ("vec", "gain", "shift") if k in s], default=-1) + 1]

    with ExitStack() as ctx:
        def sb(name, shape, dt=F32):
            return ctx.enter_context(nc.sbuf_tensor(name, shape, dt))

        ps = {(r, n): ctx.enter_context(nc.psum_tensor(f"ps_{r}{n}", [P, 512], F32))
              for r, size in RINGS.items() for n in range(size)}
        book["sems"] = {}

        def sem(name):
            book["sems"][name] = ctx.enter_context(nc.semaphore(name))
            return book["sems"][name]

        a_full, a_free, d_full, d_free, x_full, x_free = (
            sem(n) for n in ("a_full", "a_free", "d_full", "d_free", "x_full", "x_free"))
        filled = {"a": a_full, "d": d_full, "x": x_full}
        down_done = sem("down_done")
        slot_landed = [sem(f"slot_landed{n}") for n in range(SLOTS)]
        bias_landed = [sem(f"bias_landed{n}") for n in range(BIAS_SLOTS)]
        vec_landed = [sem(f"vec_landed{n}") for n in range(VEC_SLOTS)]
        x_landed, mem_landed, const_landed, small_landed, gain_landed, pe_landed = (
            sem(n) for n in ("x_landed", "mem_landed", "const_landed", "small_landed", "gain_landed", "pe_landed"))
        table_loaded, table_stored, line_stored, stored = (
            sem(n) for n in ("table_loaded", "table_stored", "line_stored", "stored"))
        dve_order, act_order, pool_order, exped, maxed = (
            sem(n) for n in ("dve_order", "act_order", "pool_order", "exped", "maxed"))

        slots = sb("slots", [P, SLOTS, SLOT])
        X = sb("X", [P, T, D])
        N = sb("N", [P, T, D])
        hT = sb("hT", [P, KD, S])
        mid = sb("mid", [P, 2560])
        proj = sb("proj", [P, T, IN_W])
        O = sb("O", [P, T, D])
        DO = sb("DO", [P, T, 512])
        bias_t = sb("bias_t", [P, BIAS_SLOTS, T, S])
        SC = sb("SC", [P, 2, T, S + 1])
        PR = sb("PR", [P, 2, T, S + 1])
        PT = sb("PT", [P, 2, 2, T, P])
        QK = sb("QK", [P, 2, 4, P])
        vec = sb("vec", [P, VEC_SLOTS, D])
        small = sb("small", [P, SV_END])
        ident = sb("ident", [P, P])
        rope_t = sb("rope_t", [P, T, 3, 2, 16])
        window = sb("window", [P, S])
        negmax = sb("negmax", [P, 4, T])
        total = sb("total", [P, 4, T])
        inv = sb("inv", [P, 4, T])
        stat = sb("stat", [P, 64])
        gate_t = sb("gate_t", [P, T, 48])

        QF = mid[:, 0:768].rearrange("p (t c) -> p t c", t=T)
        KV = mid[:, 768:1792].rearrange("p (t c) -> p t c", t=T)
        KF = mid[:, 1792:2560].rearrange("p (t c) -> p t c", t=T)
        memT = mid[:, 0:2048].rearrange("p (k s) -> p k s", k=KD)
        flat = proj[:, :, :].rearrange("p t c -> p (t c)")
        hid = flat[:, 0:2048].rearrange("p (b f s) -> p b f s", b=2, f=4)
        silu = flat[:, 2048:3072].rearrange("p (b s) -> p b s", b=2)
        logits = flat[:, 3072:3088].rearrange("p (t e) -> p t e", t=T)
        route = flat[:, 3088:3200]
        NF = N[:, :, :].rearrange("p t c -> p (t c)")
        VC = NF[:, 0:1024].rearrange("p (t c) -> p t c", t=T)
        score = NF[:, 1024:1536].rearrange("p (t s) -> p t s", t=T)
        work = NF[:, 1536:2048].rearrange("p (t s) -> p t s", t=T)
        cT = DO[:, 0, 0:S]
        KC = DO[0:HD, 0, 0:2 * CMP].rearrange("p (g n) -> p g n", g=2)
        VCMP = DO[0:CMP, 0, 32:160].rearrange("p (g n) -> p g n", g=2)
        GEL = DO[:, 0, 160:160 + 6 * 32].rearrange("p (a n) -> p a n", a=6)
        PET = DO[0:HD, 0, 352:384]
        PEN = DO[0:32, 0, 384:384 + HD]
        KPE = NF[0:HD, 0:2 * 32 * CMP].rearrange("p (g i n) -> p g i n", g=2, i=32)
        onehot = flat[0:32, 0:512]
        table = flat[0:32, 512:528]
        line_mask = flat[0:16, 1024:2048].rearrange("p (a n) -> p a n", a=2)
        lines = flat[0:16, 2048:3072].rearrange("p (a n) -> p a n", a=2)
        padded = NF[0:4 * NEAR, 0:P]
        named = {"N": N, "X": X, "O": O, "proj": proj, "QF": QF, "KV": KV, "KF": KF, "DO": DO, "hT": hT,
                 "memT": memT, "VC": VC, "logits": logits, "proj@512": proj[:, :, 512:1024],
                 "proj@1024": proj[:, :, 1024:1536], "mla_lat": proj[:, :, ML_Q:ML_Q + 384],
                 "hT2": hT[:, 2:3, :]}

        line_d = nc.dram_tensor("line_scratch", (2, 16, P, 512), F32, kind="Internal").ap()
        table_d = nc.dram_tensor("table_scratch", (DEPTH, 4 * NEAR, GRID_W, P), F32, kind="Internal").ap()

        block = ctx.enter_context(nc.Block())
        ring_first = book["ring_first"]

        def bank(lane, r):
            n = lane.ring[r]
            lane.ring[r] += 1
            return ps[r, n % RINGS[r]], n

        def emptied(lane, r, n):
            return lane.back(("free", r), n - RINGS[r], ring_first.get(r, 0), book["ring_body"].get(r, 0))

        def leave(lane, n):
            lane.mark(("done", lane.name, n))

        def experts_loop(lane):
            for r in RINGS:
                book["ring_first_new"][r] = lane.ring[r]

        def skewed(line, t):
            return bass.AP(line_d.tensor, line * P * 512 + 127 + P * (T - 1 - t), [[511, P], [1, S]])

        @block.sync
        def _(sp):
            lane = Lane(book, "sync", x_landed)
            sp.dma_start(X[:, :, :], a["x"][0].rearrange("(t p) c -> p t c", p=P)).then_inc(*lane.tick(x_landed, ("x",), by=16))

            def load(n, src):
                _, p, k, c = blocks[n]
                dst = slots[0:p, n % SLOTS, 0:k * c].rearrange("p (k c) -> p k c", k=k)
                with nc.allow_non_contiguous_dma(reason="narrow weights"):
                    sp.dma_start(dst, src).then_inc(*lane.tick(slot_landed[n % SLOTS], ("weights", n), by=16))

            end = len(blocks) if loop_first is None else loop_first
            for n in range(end):
                if n >= SLOTS:
                    sp.wait_ge(*lane.of(("used", n - SLOTS)))
                load(n, blocks[n][0])
            if loop_first is not None:
                for n in range(end - SLOTS, end):
                    sp.wait_ge(*lane.of(("used", n)))
                body = len(blocks) - end
                whole = a["moe_w_gate_2"][0], a["moe_w_up_2"][0], a["moe_w_down_2"][0]
                with lane.loop(sp, EXPERTS // BODY) as turn:
                    n = end
                    for u in range(BODY):
                        e = turn * BODY + u
                        gate, up = (w[bass.ds(e, 1)].rearrange("e (k p) c -> p (e k) c", p=P) for w in whole[:2])
                        groups = expert_stage[0][1]["groups"][u]
                        order = []
                        for g, group in enumerate(groups):
                            c0 = 512 * g
                            order.append((group["gate"], gate[:, :, c0:c0 + 512]))
                            order.append((group["up"], up[:, :, c0:c0 + 512]))
                            order.append((group["down"], whole[2][bass.ds(e, 1), c0:c0 + 512, :].rearrange(
                                "e (k p) c -> p (e k) c", p=P)))
                        for n, src in sorted(order, key=lambda x: x[0]):
                            sp.wait_ge(*lane.back(("used",), n - SLOTS, end, body))
                            load(n, src)
            sp.wait_ge(*lane.of(("done", "vector", len(stages) - 2)))
            sp.dma_start(out[0].rearrange("(t p) c -> p t c", p=P), X[:, :, :]).then_inc(*lane.tick(stored, ("stored",), by=16))
            sp.wait_ge(*lane.own())

        @block.gpsimd
        def _(pool):
            lane = Lane(book, "gpsimd", x_landed)
            with nc.allow_non_contiguous_dma(reason="small tables"):
                for dst, src in ((ident[:, :], a["c_ident"]), (window[:, :], a["c_window"]),
                                 (rope_t[:, :, :, :, :].rearrange("p t a b c -> p t (a b c)"),
                                  a["c_rope"].rearrange("(t p) a b c -> p t (a b c)", p=P)),
                                 (onehot, a["c_bucket"]), (table, a["rel_table_2"]),
                                 (line_mask, a["c_line"].unsqueeze(0).broadcast_to([16, 2, 512]))):
                    pool.dma_start(dst, src).then_inc(*lane.tick(const_landed, ("const",), by=16))
                for l in range(DEPTH):
                    if l:
                        pool.wait_ge(*lane.of(("table_stored", l - 1)))
                    pool.memset(padded, 0.0).then_inc(*lane.tick(pool_order))
                    pool.wait_ge(*lane.own())
                    for h in range(4):
                        pool.dma_start(padded[NEAR * h:NEAR * h + NEAR, 48:79],
                                                   a["na_rel_bias"][l, h, NA_ROWS - ROWS:NA_ROWS - ROWS + NEAR, :]).then_inc(*lane.tick(table_loaded, by=16))
                    pool.wait_ge(*lane.own())
                    pool.dma_start(table_d[l], padded.unsqueeze(1).broadcast_to([4 * NEAR, GRID_W, P])).then_inc(*lane.tick(table_stored, ("table_stored", l), by=16))
                pool.wait_ge(*lane.of(("table_stored", DEPTH - 1)))
                pool.wait_ge(*lane.of(("lines",)))
                for v, h0 in ((0, 0), (1, 8)):
                    pool.dma_start(line_d[v, h0:16], lines[h0:16, v, :].unsqueeze(1).broadcast_to(
                        [16 - h0, P, 512])).then_inc(*lane.tick(line_stored, ("line_stored",), by=16))

                todo = []
                for n, (kind, s) in enumerate(stages):
                    if kind == "small":
                        todo.append(("small", n, s["l"]))
                    if kind == "load_mem":
                        todo.append(("mem", n, None))
                    if kind == "latent_norm":
                        todo.append(("latent", n, None))
                    if kind == "compress":
                        todo.append(("pe", n, s["n"]))
                    for k in ("vec", "gain", "shift"):
                        if k in s:
                            todo.append(("vec", n, s[k]))
                    if kind == "select":
                        todo.append(("bias", n, s["bias"]))
                    if kind == "route":
                        todo.append(("index", n, None))
                    for b in sorted({j["bias"] for j in s.get("jobs", []) if j["bias"] is not None}):
                        todo.append(("bias", n, b))

                def spread(src):
                    return src.unsqueeze(0).broadcast_to([P, src.shape[0]])

                for what, n, m in todo:
                    if what == "small":
                        if m:
                            pool.wait_ge(*lane.of(("diff", m - 1)))
                        for at, src in ((SV_GQ, a["gqa_q_norm"]), (SV_GK, a["gqa_k_norm"]), (SV_MQ, a["mla_q_norm"]),
                                        (SV_MKV, a["mla_kv_norm"]), (SV_SUB, a["diff_subln"]),
                                        (SV_LAM, a["diff_lambda_q1"]), (SV_LAM + 32, a["diff_lambda_k1"]),
                                        (SV_LAM + 64, a["diff_lambda_q2"]), (SV_LAM + 96, a["diff_lambda_k2"])):
                            pool.dma_start(small[:, at:at + src.shape[1]], spread(src[m])).then_inc(*lane.tick(small_landed, ("small", m), by=16))
                    elif what == "mem":
                        pool.wait_ge(*lane.of(("done", "vector", n - 1)))
                        pool.dma_start(N[:, :, :], a["mem_2"][0].rearrange("(t p) c -> p t c", p=P)).then_inc(*lane.tick(mem_landed, ("mem",), by=16))
                    elif what == "latent":
                        pool.wait_ge(*lane.of(("diff", DEPTH - 1)))
                        pool.dma_start(small[:, 0:P], spread(a["ev_ckv_gain_2"][0])).then_inc(*lane.tick(gain_landed, ("latent",), by=16))
                        pool.dma_start(small[:, P:P + 8], spread(a["ev_sinks_2"][0])).then_inc(*lane.tick(gain_landed, ("latent",), by=16))
                    elif what == "index":
                        pool.wait_ge(*lane.of(("done", "vector", n - 2)))
                        pool.dma_start(small[:, 0:8], spread(a["c_index"][0])).then_inc(*lane.tick(gain_landed, ("index",), by=16))
                    elif what == "pe":
                        pool.wait_ge(*lane.of(("done", "vector", n - 1)))
                        pool.wait_ge(*lane.of(("done", "tensor", n - 1)))
                        pool.dma_start(PEN, a["od_pe_k_2" if m == 0 else "od_pe_v_2"][0]).then_inc(*lane.tick(pe_landed, ("pe", m), by=16))
                    elif what == "vec":
                        if m >= VEC_SLOTS:
                            pool.wait_ge(*lane.of(("vec_used", m - VEC_SLOTS)))
                        pool.dma_start(vec[:, m % VEC_SLOTS, :], spread(vectors[m])).then_inc(*lane.tick(vec_landed[m % VEC_SLOTS], ("vec", m), by=16))
                    else:
                        kind, *where = biases[m]
                        landed = bias_landed[m % BIAS_SLOTS]
                        tile = bias_t[:, m % BIAS_SLOTS]
                        if m >= BIAS_SLOTS:
                            pool.wait_ge(*lane.of(("bias_used", m - BIAS_SLOTS)))
                        if kind == "na":
                            l, h = where
                            for t in range(T):
                                for half in range(P // GRID_W):
                                    row = T * t + half
                                    src = bass.AP(table_d.tensor,
                                                  ((l * 4 + h) * NEAR + ROWS - 1 - row) * GRID_W * P + GRID_W - 1,
                                                  [[P - 1, GRID_W], [GRID_W * P, ROWS], [1, GRID_W]])
                                    dst = tile[GRID_W * half:GRID_W * half + GRID_W, t, :].rearrange(
                                        "p (r c) -> p r c", r=ROWS)
                                    pool.dma_start(dst, src).then_inc(*lane.tick(landed, by=16))
                            pool.wait_ge(*lane.own())
                            pool.tensor_tensor(
                                tile, tile, window[:, :].unsqueeze(1).broadcast_to([P, T, S]), ALU.add).then_inc(*lane.tick(pool_order, ("bias", m)))
                        elif kind in ("alibi", "line"):
                            src = a["c_alibi"][where[0]] if kind == "alibi" else a["c_causal"]
                            pool.dma_start(tile, src.rearrange("(t p) k -> p t k", p=P)).then_inc(*lane.tick(landed, ("bias", m), by=16))
                        else:
                            pool.wait_ge(*lane.of(("line_stored",)))
                            for t in range(T):
                                pool.dma_start(tile[:, t, :], skewed(
                                    16 * (kind == "band") + where[0], t)).then_inc(*lane.tick(landed, ("bias", m), by=16))

        @block.tensor
        def _(pe):
            lane = Lane(book, "tensor", x_landed)
            state = {"group": 0, "pair": 0}

            def slot(n):
                pe.wait_ge(*lane.of(("weights", n)))
                _, p, k, c = blocks[n]
                return slots[0:p, n % SLOTS, 0:k * c].rearrange("p (k c) -> p k c", k=k)

            def turn(s):
                src, dst = named[s["src"]], s["chunks"]
                for k0 in range(0, dst, 2):
                    b, n = bank(lane, "a")
                    pe.wait_ge(*emptied(lane, "a", n))
                    ks = range(k0, min(k0 + 2, dst))
                    for k in ks:
                        for t in range(T):
                            o = ((k - k0) * T + t) * P
                            last = pe.transpose(b[:, o:o + P], src[:, t, k * P:(k + 1) * P], ident[:, :])
                    last.then_inc(*lane.tick(a_full, ("full", "a", n)))

            def linear(s):
                lhs = named[s["lhs"]]
                for w, _, c in s["blocks"]:
                    v = slot(w)
                    for t in range(T):
                        for j in range(0, c, 512):
                            b, n = bank(lane, "a")
                            pe.wait_ge(*emptied(lane, "a", n))
                            width = min(512, c - j)
                            for k in range(s["k"]):
                                last = pe.matmul(b[:, 0:width], lhs[:, k, t * P:(t + 1) * P], v[:, k, j:j + width],
                                                 start=(k == 0), stop=(k == s["k"] - 1))
                            last.then_inc(*lane.tick(a_full, ("full", "a", n), ("used", w)))

            def attend(s, stage_n):
                jobs = s["jobs"]
                count = len(jobs)

                def heads(i):
                    j = jobs[i]
                    if "q" not in j:
                        return
                    b, n = bank(lane, "a")
                    pe.wait_ge(*emptied(lane, "a", n))
                    parts = [j["q"]] + ([j["k"]] if "k" in j else [])
                    for m, (name, c) in enumerate(parts):
                        for t in range(T):
                            last = pe.transpose(b[0:j["d"], (m * T + t) * P:(m * T + t + 1) * P],
                                                named[name][:, t, c:c + j["d"]], ident[:, :])
                    last.then_inc(*lane.tick(a_full, ("full", "a", n)))

                def scores(i):
                    j = jobs[i]
                    d, keys = j["d"], j.get("keys", S)
                    if "q" in j:
                        pe.wait_ge(*lane.of(("heads", stage_n, i)))
                        qT = QK[0:d, i % 2, 0:2, :].rearrange("p a n -> p (a n)")
                    else:
                        qT = hT[:, j["qT"][1], :]
                    if "k" in j:
                        kT = QK[0:d, i % 2, 2:4, :].rearrange("p a n -> p (a n)")
                    else:
                        kT = cT if j["kT"] == "cT" else KC[:, j["kT"][1], :]
                    b, n = bank(lane, "d")
                    pe.wait_ge(*emptied(lane, "d", n))
                    for t in range(T):
                        last = pe.matmul(b[:, t * keys:(t + 1) * keys], qT[:, t * P:(t + 1) * P], kT,
                                         start=True, stop=True)
                    last.then_inc(*lane.tick(d_full, ("full", "d", n), ("scores", stage_n, i)))

                def turn_probs(i):
                    j = jobs[i]
                    keys = j.get("keys", S)
                    pe.wait_ge(*lane.of(("probs", stage_n, i)))
                    b, n = bank(lane, "a")
                    pe.wait_ge(*emptied(lane, "a", n))
                    for kc in range(-(-keys // P)):
                        w = min(P, keys - kc * P)
                        for t in range(T):
                            last = pe.transpose(b[0:w, (kc * T + t) * P:(kc * T + t + 1) * P],
                                                PR[:, i % 2, t, kc * P:kc * P + w], ident[:, :])
                    last.then_inc(*lane.tick(a_full, ("full", "a", n), ("probs_turned", stage_n, i)))

                def values(i):
                    j = jobs[i]
                    keys, dv = j.get("keys", S), j["dv"]
                    pe.wait_ge(*lane.of(("pt", stage_n, i)))
                    b, n = bank(lane, "x")
                    pe.wait_ge(*emptied(lane, "x", n))
                    chunks = -(-keys // P)
                    for t in range(T):
                        for kc in range(chunks):
                            w = min(P, keys - kc * P)
                            v = VCMP[:, j["v"][1], :] if j["v"][0] == "VCMP" else \
                                named[j["v"][0]][:, kc, j["v"][1]:j["v"][1] + dv]
                            last = pe.matmul(b[:, t * dv:(t + 1) * dv], PT[0:w, i % 2, kc, t, :], v,
                                             start=(kc == 0), stop=(kc == chunks - 1))
                    last.then_inc(*lane.tick(x_full, ("full", "x", n), ("values", stage_n, i)))

                for i in range(count + 4):
                    if i < count:
                        heads(i)
                    if 0 <= i - 1 < count:
                        scores(i - 1)
                    if 0 <= i - 3 < count:
                        turn_probs(i - 3)
                    if 0 <= i - 4 < count:
                        values(i - 4)

            def gate_up(group):
                gv, uv = slot(group["gate"]), slot(group["up"])
                for f0 in range(0, group["w"] // P, 2):
                    for w, v, r in (("gate", gv, "a"), ("up", uv, "d")):
                        b, n = bank(lane, r)
                        pe.wait_ge(*emptied(lane, r, n))
                        for f in range(2):
                            for k in range(KD):
                                last = pe.matmul(b[:, f * S:(f + 1) * S], v[:, k, (f0 + f) * P:(f0 + f + 1) * P],
                                                 hT[:, k, :], start=(k == 0), stop=(k == KD - 1))
                        last.then_inc(*lane.tick(filled[r], ("full", r, n), ("used", group[w])))
                    state["pair"] += 1
                group_pair = state["pair"] - 1
                return group_pair

            def down(group, n_group, pair, accs, first, final):
                v = slot(group["down"])
                nf = group["w"] // P
                for f in range(nf):
                    if f % 2 == 0:
                        pe.wait_ge(*lane.of(("hidden", pair - (nf - 1) // 2 + f // 2)))
                    for t in range(T):
                        for half in range(2):
                            b, n = accs[2 * t + half]
                            start, stop = first and f == 0, final and f == nf - 1
                            last = pe.matmul(b[:, :], hid[:, n_group % 2, f, t * P:(t + 1) * P],
                                             v[:, f, half * 512:(half + 1) * 512], start=start, stop=stop)
                            if stop:
                                last.then_inc(*lane.tick(x_full, ("full", "x", n)))
                if final:
                    lane.mark(("down", n_group), ("used", group["down"]))
                else:
                    last.then_inc(*lane.tick(down_done, ("down", n_group), ("used", group["down"])))

            def ffn(groups):
                late, accs = None, None
                for g, group in enumerate(groups):
                    pair = gate_up(group)
                    n_group = state["group"]
                    state["group"] += 1
                    if late is not None:
                        if accs is None:
                            accs = [bank(lane, "x") for _ in range(4)]
                            for _, n in accs:
                                pe.wait_ge(*emptied(lane, "x", n))
                        down(*late, accs, g == 1, False)
                    late = (group, n_group, pair)
                down(*late, accs, False, True)

            def small_turn(parts, width):
                b, n = bank(lane, "a")
                pe.wait_ge(*emptied(lane, "a", n))
                for m, piece in enumerate(parts):
                    last = pe.transpose(b[0:width, m * P:(m + 1) * P], piece, ident[:, :])
                last.then_inc(*lane.tick(a_full, ("full", "a", n)))

            def index_scores(stage_n):
                for pair in range(4):
                    small_turn([proj[:, t, 640 + HD * h:704 + HD * h] for h in (2 * pair, 2 * pair + 1)
                                for t in range(T)], HD)
                small_turn([proj[:, t, 1152:1216] for t in range(T)], HD)
                pe.wait_ge(*lane.of(("index_turned", stage_n)))
                for h in range(8):
                    b, n = bank(lane, "a")
                    pe.wait_ge(*emptied(lane, "a", n))
                    for t in range(T):
                        last = pe.matmul(b[:, t * S:(t + 1) * S], hT[0:HD, h, t * P:(t + 1) * P],
                                         QK[0:HD, 0, 0:2, :].rearrange("p a n -> p (a n)"), start=True, stop=True)
                    last.then_inc(*lane.tick(a_full, ("full", "a", n)))

            def latent_heads(s, stage_n):
                small_turn([proj[:, t, 512:640] for t in range(T)], P)
                for pair in range(4):
                    small_turn([proj[:, t, HD * h:HD * h + HD] for h in (2 * pair, 2 * pair + 1) for t in range(T)],
                               HD)
                    pe.wait_ge(*lane.of(("latent_turned", pair)))
                    uk = slot(s["uk"])
                    b, n = bank(lane, "a")
                    pe.wait_ge(*emptied(lane, "a", n))
                    for m in range(2):
                        last = pe.matmul(b[:, m * S:(m + 1) * S], uk[:, 2 * pair + m, :],
                                         QK[0:HD, pair % 2, 2 * m:2 * m + 2, :].rearrange("p a n -> p (a n)"),
                                         start=True, stop=True)
                    last.then_inc(*lane.tick(a_full, ("full", "a", n), ("used", s["uk"]), ("latent_scored", pair)))
                uv = slot(s["uv"]).rearrange("p k c -> p (k c)")
                for t in range(T):
                    b, n = bank(lane, "a")
                    pe.wait_ge(*emptied(lane, "a", n))
                    pe.matmul(b[:, :], cT[:, t * P:(t + 1) * P], uv, start=True, stop=True).then_inc(*lane.tick(a_full, ("full", "a", n), ("used", s["uv"])))

            def compress(s, stage_n):
                base = 1024 + P * s["n"]
                small_turn([proj[:, t, base + HD * g:base + HD * g + HD] for g in range(2) for t in range(T)], HD)
                pe.wait_ge(*lane.of(("pe", s["n"])))
                b, n = bank(lane, "a")
                pe.wait_ge(*emptied(lane, "a", n))
                pe.transpose(b[0:HD, 0:32], PEN, ident[0:32, 0:32]).then_inc(*lane.tick(a_full, ("full", "a", n)))
                pe.wait_ge(*lane.of(("blocks", s["n"])))
                w1 = slot(s["w1"])
                b, n = bank(lane, "d")
                pe.wait_ge(*emptied(lane, "d", n))
                for i in range(32):
                    last = pe.matmul(b[:, 0:2 * CMP], w1[:, i, :], KPE[:, :, i, :], start=(i == 0), stop=(i == 31))
                last.then_inc(*lane.tick(d_full, ("full", "d", n), ("used", s["w1"])))
                pe.wait_ge(*lane.of(("gelu", s["n"])))
                w2 = slot(s["w2"])
                b, n = bank(lane, "a")
                pe.wait_ge(*emptied(lane, "a", n))
                if s["n"] == 0:
                    last = pe.matmul(b[0:HD, 0:2 * CMP], w2[:, 0, :], GEL[:, 5, 0:2 * CMP], start=True, stop=True)
                else:
                    for g in range(2):
                        last = pe.matmul(b[0:CMP, g * HD:(g + 1) * HD], GEL[:, 5, g * CMP:(g + 1) * CMP],
                                         w2[:, 0, :], start=True, stop=True)
                last.then_inc(*lane.tick(a_full, ("full", "a", n), ("used", s["w2"])))

            for n, (kind, s) in enumerate(stages):
                if kind == "lines":
                    pe.wait_ge(*lane.of(("const",)))
                    b, m = bank(lane, "d")
                    pe.wait_ge(*emptied(lane, "d", m))
                    pe.matmul(b[0:16, :], table, onehot, start=True, stop=True).then_inc(*lane.tick(d_full, ("full", "d", m)))
                elif kind in ("turn", "linear", "attend", "ffn", "index_scores", "latent_heads", "compress", "experts"):
                    pe.wait_ge(*lane.of(("done", "scalar", n - 1)))
                    pe.wait_ge(*lane.of(("done", "vector", n - 1)))
                    pe.wait_ge(*lane.of(("done", "gpsimd", n - 1)))
                if kind == "turn":
                    if s["dst"] == "memT":
                        pe.wait_ge(*lane.of(("mem",)))
                    turn(s)
                elif kind == "linear":
                    linear(s)
                elif kind == "attend":
                    attend(s, n)
                elif kind == "ffn":
                    ffn(s["groups"])
                elif kind == "index_scores":
                    index_scores(n)
                elif kind == "latent_heads":
                    latent_heads(s, n)
                elif kind == "compress":
                    compress(s, n)
                elif kind == "experts":
                    experts_loop(lane)
                    before = dict(lane.ring)
                    with lane.loop(pe, EXPERTS // BODY):
                        for groups in s["groups"]:
                            ffn(groups)
                    for r in RINGS:
                        book["ring_body_new"][r] = lane.ring[r] - before[r]
                leave(lane, n)

        @block.scalar
        def _(act):
            lane = Lane(book, "scalar", x_landed)
            state = {"pair": 0, "root": 0}

            def root():
                r = state["root"]
                state["root"] += 1
                act.wait_ge(*lane.of(("variance", r)))
                w = book["width"].get(r, 1)
                act.activation(stat[:, 0:w], stat[:, 0:w], ACT.Sqrt).then_inc(*lane.tick(act_order, ("root", r)))

            def turn(s):
                dst = named[s["dst"]]
                for k0 in range(0, s["chunks"], 2):
                    b, n = bank(lane, "a")
                    act.wait_ge(*lane.of(("full", "a", n)))
                    w = min(2, s["chunks"] - k0)
                    act.activation(dst[:, k0:k0 + w, :].rearrange("p k s -> p (k s)"), b[:, 0:w * S], ACT.Copy).then_inc(*lane.tick(a_free, ("free", "a", n)))

            def linear(s):
                dst = named[s["dst"]]
                for _, c0, c in s["blocks"]:
                    for t in range(T):
                        for j in range(0, c, 512):
                            b, n = bank(lane, "a")
                            act.wait_ge(*lane.of(("full", "a", n)))
                            w = min(512, c - j)
                            act.activation(dst[:, t, c0 + j:c0 + j + w], b[:, 0:w], ACT.Copy).then_inc(*lane.tick(a_free, ("free", "a", n)))

            def attend(s, stage_n):
                jobs = s["jobs"]
                count = len(jobs)

                def heads(i):
                    j = jobs[i]
                    if "q" not in j:
                        return
                    b, n = bank(lane, "a")
                    act.wait_ge(*lane.of(("full", "a", n)))
                    if i >= 2:
                        act.wait_ge(*lane.of(("scores", stage_n, i - 2)))
                    w = 4 if "k" in j else 2
                    act.activation(QK[0:j["d"], i % 2, 0:w, :].rearrange("p a n -> p (a n)"),
                                         b[0:j["d"], 0:w * P], ACT.Copy).then_inc(*lane.tick(a_free, ("free", "a", n), ("heads", stage_n, i)))

                def exps(i):
                    j = jobs[i]
                    keys = j.get("keys", S) + ("sink" in j)
                    act.wait_ge(*lane.of(("max", stage_n, i)))
                    if i >= 2:
                        act.wait_ge(*lane.of(("probs_turned", stage_n, i - 2)))
                    if i >= 4:
                        act.wait_ge(*lane.of(("normed", stage_n, i - 4)))
                    for t in range(T):
                        act.activation(PR[:, i % 2, t, 0:keys], SC[:, i % 2, t, 0:keys], ACT.Exp,
                                                   bias=negmax[:, i % 4, t:t + 1], accum_out=total[:, i % 4, t:t + 1]).then_inc(*lane.tick(exped, ("probs", stage_n, i)))

                def turned(i):
                    keys = jobs[i].get("keys", S)
                    b, n = bank(lane, "a")
                    act.wait_ge(*lane.of(("full", "a", n)))
                    if i >= 2:
                        act.wait_ge(*lane.of(("values", stage_n, i - 2)))
                    w = min(P, keys)
                    m = -(-keys // P)
                    act.activation(PT[0:w, i % 2, 0:m].rearrange("p k t n -> p (k t n)"), b[0:w, 0:m * T * P],
                                         ACT.Copy).then_inc(*lane.tick(a_free, ("free", "a", n), ("pt", stage_n, i)))

                for i in range(count + 4):
                    if i < count:
                        heads(i)
                    if 0 <= i - 2 < count:
                        exps(i - 2)
                    if 0 <= i - 3 < count:
                        turned(i - 3)

            def ffn(groups):
                for group in groups:
                    for _ in range(group["w"] // P // 2):
                        b, n = bank(lane, "a")
                        act.wait_ge(*lane.of(("full", "a", n)))
                        p = state["pair"]
                        state["pair"] += 1
                        act.wait_ge(*lane.back(("hidden",), p - 2, book["pair_first"], book["pair_body"]))
                        act.activation(silu[:, p % 2, :], b[:, :], ACT.Silu).then_inc(*lane.tick(a_free, ("free", "a", n), ("silu", p)))

            def plain(dst, w, parts=P, *keys, func=ACT.Copy, scale=1.0):
                b, n = bank(lane, "a")
                act.wait_ge(*lane.of(("full", "a", n)))
                act.activation(dst, b[0:parts, 0:w], func, scale=scale).then_inc(*lane.tick(a_free, ("free", "a", n), *keys))

            for n, (kind, s) in enumerate(stages):
                if kind in ("turn", "linear", "attend", "ffn", "experts", "index_scores", "latent_heads",
                            "compress", "gates", "route", "diff_out"):
                    act.wait_ge(*lane.of(("done", "tensor", n - 1)))
                    act.wait_ge(*lane.of(("done", "vector", n - 1)))
                    act.wait_ge(*lane.of(("done", "gpsimd", n - 1)))
                if kind == "turn":
                    turn(s)
                elif kind == "linear":
                    linear(s)
                elif kind == "attend":
                    attend(s, n)
                elif kind in ("rms_pre", "rms_add", "layer_norm", "latent_norm"):
                    root()
                elif kind == "head_norms":
                    root()
                elif kind == "diff_out":
                    act.wait_ge(*lane.of(("lambda", s["l"])))
                    act.activation(stat[:, 0:2], stat[:, 0:2], ACT.Exp).then_inc(*lane.tick(act_order, ("lambda_exp", s["l"])))
                    root()
                elif kind == "ffn":
                    ffn(s["groups"])
                elif kind == "index_scores":
                    for pair in range(4):
                        plain(hT[0:HD, 2 * pair:2 * pair + 2, :].rearrange("p k s -> p (k s)"), 512, HD)
                    plain(QK[0:HD, 0, 0:2, :].rearrange("p a n -> p (a n)"), S, HD, ("index_turned", n))
                    for h in range(8):
                        if h >= 2:
                            act.wait_ge(*lane.of(("indexed", h - 2)))
                        plain(SC[:, h % 2, :, 0:S], 512, P, ("relu", h), func=ACT.Relu, scale=HD ** -0.5)
                elif kind == "latent_heads":
                    plain(cT, S)
                    for pair in range(4):
                        if pair >= 2:
                            act.wait_ge(*lane.of(("latent_scored", pair - 2)))
                        plain(QK[0:HD, pair % 2, :, :].rearrange("p a n -> p (a n)"), 512, HD, ("latent_turned", pair))
                        plain(hT[:, 2 * pair:2 * pair + 2, :].rearrange("p k s -> p (k s)"), 512)
                    for t in range(T):
                        plain(VC[:, t, :], 512)
                elif kind == "gates":
                    act.wait_ge(*lane.own())
                    act.activation(gate_t[:, :, :], proj[:, :, 1792:1840], ACT.Exp, scale=-1.0).then_inc(*lane.tick(act_order, ("gate_exp",)))
                elif kind == "compress":
                    plain(QK[0:HD, 0, :, :].rearrange("p a n -> p (a n)"), 512, HD)
                    plain(PET, 32, HD, ("compress_turned", s["n"]))
                    act.wait_ge(*lane.of(("gelu_arg", s["n"])))
                    act.activation(GEL[:, 4, 0:2 * CMP], GEL[:, 3, 0:2 * CMP], ACT.Exp,
                                               scale=-2.0 * math.sqrt(2.0 / math.pi)).then_inc(*lane.tick(act_order, ("gelu_exp", s["n"])))
                    if s["n"] == 0:
                        plain(KC.rearrange("p g n -> p (g n)"), 2 * CMP, HD)
                    else:
                        plain(VCMP.rearrange("p g n -> p (g n)"), 2 * HD, CMP)
                elif kind == "route":
                    act.wait_ge(*lane.of(("route_arg",)))
                    act.activation(route[:, 32:34], route[:, 32:34], ACT.Exp).then_inc(*lane.tick(act_order, ("route_exp",)))
                elif kind == "experts":
                    book["pair_first_new"] = state["pair"]
                    with lane.loop(act, EXPERTS // BODY):
                        for groups in s["groups"]:
                            ffn(groups)
                    book["pair_body_new"] = state["pair"] - book["pair_first_new"]
                leave(lane, n)

        @block.vector
        def _(dve):
            lane = Lane(book, "vector", x_landed)
            state = {"pair": 0, "root": 0, "group": 0}

            def do(ins, *keys, sem=dve_order):
                ins.then_inc(*lane.tick(sem, *keys))
                dve.wait_ge(*lane.own())

            def post(ins, *keys, sem=dve_order):
                ins.then_inc(*lane.tick(sem, *keys))

            def inv_root(width, source, scale, eps):
                r = state["root"]
                state["root"] += 1
                book["width"][r] = width
                do(dve.tensor_scalar(stat[:, 0:width], source, scale, eps, ALU.mult, ALU.add), ("variance", r))
                dve.wait_ge(*lane.of(("root", r)))
                do(dve.reciprocal(stat[:, 0:width], stat[:, 0:width]))

            def squares(src, width, scratch):
                for t in range(T):
                    do(dve.tensor_tensor_reduce(scratch[:, t, 0:width], src[:, t, :], src[:, t, :], 1.0, 0.0,
                                                ALU.mult, ALU.add, stat[:, 32 + t:33 + t]))

            def use_vec(m):
                dve.wait_ge(*lane.of(("vec", m)))
                return vec[:, m % VEC_SLOTS, :]

            def rms_pre(s):
                squares(X, D, N)
                inv_root(T, stat[:, 32:34], 1.0 / D, EPS)
                w = use_vec(s["vec"])
                for t in range(T):
                    post(dve.scalar_tensor_tensor(N[:, t, :], X[:, t, :], stat[:, t:t + 1], w, ALU.mult, ALU.mult),
                         ("vec_used", s["vec"]))

            def rms_add(s):
                squares(N, D, O)
                inv_root(T, stat[:, 32:34], 1.0 / D, EPS)
                w = use_vec(s["vec"])
                for t in range(T):
                    do(dve.scalar_tensor_tensor(N[:, t, :], N[:, t, :], stat[:, t:t + 1], w, ALU.mult, ALU.mult),
                       ("vec_used", s["vec"]))
                    do(dve.tensor_tensor(X[:, t, :], X[:, t, :], N[:, t, :], ALU.add))

            def layer_norm(s):
                g, b = use_vec(s["gain"]), use_vec(s["shift"])
                for t in range(T):
                    do(dve.scalar_tensor_tensor(X[:, t, :], X[:, t, :], ALPHA, N[:, t, :], ALU.mult, ALU.add))
                    for c in range(2):
                        do(dve.bn_stats(stat[:, 36 + 6 * c:42 + 6 * c], X[:, t, 512 * c:512 * c + 512]))
                    do(dve.bn_aggr(stat[:, 32 + 2 * t:34 + 2 * t], stat[:, 36:48]))
                inv_root(T, stat[:, 33:36:2], 1.0, LN_EPS)
                for t in range(T):
                    do(dve.tensor_scalar(X[:, t, :], X[:, t, :], stat[:, 32 + 2 * t:33 + 2 * t], stat[:, t:t + 1],
                                         ALU.subtract, ALU.mult))
                    do(dve.tensor_tensor(X[:, t, :], X[:, t, :], g, ALU.mult), ("vec_used", s["gain"]))
                    do(dve.tensor_tensor(X[:, t, :], X[:, t, :], b, ALU.add), ("vec_used", s["shift"]))

            def rope(x, cos, sin):
                shape = [P, x.shape[1], x.shape[2], 16]
                size = shape[1] * shape[2] * 16
                x1, x2 = x[:, :, :, 0, :], x[:, :, :, 1, :]
                c, s = cos.unsqueeze(1).broadcast_to(shape), sin.unsqueeze(1).broadcast_to(shape)
                tmp = [SC[:, m // 2, m % 2, 0:size].rearrange("p (h b c) -> p h b c", h=shape[1], b=shape[2])
                       for m in range(4)]
                for m, (u, v) in enumerate(((x1, c), (x2, s), (x2, c), (x1, s))):
                    do(dve.tensor_tensor(tmp[m], u, v, ALU.mult))
                do(dve.tensor_tensor(x1, tmp[0], tmp[1], ALU.subtract))
                do(dve.tensor_tensor(x2, tmp[2], tmp[3], ALU.add))

            def head_norms(s):
                dve.wait_ge(*lane.of(("small", s["l"])))
                gq = proj[:, :, GQ_Q:GQ_V].rearrange("p t (h c) -> p t h c", h=6)
                for t in range(T):
                    sq = PR[:, t, :, 0:192].rearrange("p a c -> p a c")
                    x = proj[:, t, GQ_Q:GQ_V].rearrange("p (a c) -> p a c", a=2)
                    do(dve.tensor_tensor(sq, x, x, ALU.mult))
                    for half in range(2):
                        do(dve.tensor_reduce(stat[:, 32 + 6 * t + 3 * half:35 + 6 * t + 3 * half],
                                             PR[:, t, half, 0:192].rearrange("p (h c) -> p h c", h=3), AX, ALU.add))
                    for n, (c0, w) in enumerate(((ML_Q, 256), (ML_KV, 128))):
                        x = proj[:, t, c0:c0 + w]
                        do(dve.tensor_tensor_reduce(PR[:, t, 0, 0:w], x, x, 64.0 / w, 0.0, ALU.mult, ALU.add,
                                                    stat[:, 44 + 2 * t + n:45 + 2 * t + n]))
                inv_root(16, stat[:, 32:48], 1.0 / HD, EPS)
                for t in range(T):
                    x = gq[:, t]
                    do(dve.tensor_tensor(x, x, stat[:, 6 * t:6 * t + 6].unsqueeze(2).broadcast_to([P, 6, HD]), ALU.mult))
                    for h0, h1, at in ((0, 4, SV_GQ), (4, 6, SV_GK)):
                        w = small[:, at:at + HD].unsqueeze(1).broadcast_to([P, h1 - h0, HD])
                        do(dve.tensor_tensor(x[:, h0:h1, :], x[:, h0:h1, :], w, ALU.mult))
                    for n, (c0, w, at) in enumerate(((ML_Q, 256, SV_MQ), (ML_KV, 128, SV_MKV))):
                        x = proj[:, t, c0:c0 + w]
                        do(dve.scalar_tensor_tensor(x, x, stat[:, 12 + 2 * t + n:13 + 2 * t + n], small[:, at:at + w],
                                                    ALU.mult, ALU.mult))
                    rope(proj[:, t, GQ_Q:GQ_V].rearrange("p (h b a c) -> p h b a c", h=6, b=2, a=2),
                         rope_t[:, t, 0:2, 0, :], rope_t[:, t, 0:2, 1, :])

            def mla_keys():
                for t in range(T):
                    kr = proj[:, t, ML_KR:ML_KR + 32].rearrange("p (h b a c) -> p h b a c", h=1, b=1, a=2)
                    cos, sin = rope_t[:, t, 2:3, 0, :], rope_t[:, t, 2:3, 1, :]
                    rope(kr, cos, sin)
                    q = QF[:, t, :].rearrange("p (h c) -> p h c", h=4)[:, :, 64:96]
                    rope(q.unsqueeze(2).rearrange("p h b (a c) -> p h b a c", a=2), cos, sin)
                    k = KF[:, t, :].rearrange("p (h c) -> p h c", h=4)
                    do(dve.tensor_copy(k[:, :, 0:64], KV[:, t, :].rearrange("p (h c) -> p h c", h=4)[:, :, 0:64]))
                    do(dve.tensor_copy(k[:, :, 64:96], proj[:, t, ML_KR:ML_KR + 32].unsqueeze(1).broadcast_to(
                        [P, 4, 32])))

            def attend(s, stage_n):
                jobs = s["jobs"]
                count = len(jobs)

                def scores(i):
                    j = jobs[i]
                    keys = j.get("keys", S)
                    b, n = bank(lane, "d")
                    dve.wait_ge(*lane.of(("full", "d", n)))
                    if i >= 2:
                        dve.wait_ge(*lane.of(("probs", stage_n, i - 2)))
                    got = b[:, 0:T * keys].rearrange("p (t k) -> p t k", t=T)
                    sc = SC[:, i % 2, :, 0:keys]
                    if j["bias"] is None:
                        do(dve.tensor_scalar(sc, got, j["scale"], None, ALU.mult), ("free", "d", n), sem=d_free)
                    else:
                        dve.wait_ge(*lane.of(("bias", j["bias"])))
                        tile = bias_t[:, j["bias"] % BIAS_SLOTS]
                        if j.get("selected"):
                            do(dve.tensor_tensor(tile, tile, score, ALU.add))
                        if keys != S:
                            tile = tile[:, :, 31:31 + 16 * (CMP - 1) + 1:16]
                        do(dve.scalar_tensor_tensor(sc, got, j["scale"], tile, ALU.mult, ALU.add),
                           ("free", "d", n), *([("bias_used", j["bias"])] if j["bias_last"] else []), sem=d_free)
                    width = keys
                    if "sink" in j:
                        width += 1
                        do(dve.tensor_copy(SC[:, i % 2, :, keys:keys + 1],
                                           small[:, P + j["sink"]:P + j["sink"] + 1].unsqueeze(1).broadcast_to(
                                               [P, T, 1])))
                    nm = negmax[:, i % 4, :]
                    last = dve.tensor_reduce(nm, SC[:, i % 2, :, 0:width], AX, ALU.max, negate=True)
                    if keys != S:
                        do(last)
                        last = dve.tensor_scalar(nm, nm, 1e20, None, ALU.min)
                    post(last, ("max", stage_n, i), sem=maxed)

                def normed(i):
                    j = jobs[i]
                    dv = j["dv"]
                    dve.wait_ge(*lane.of(("probs", stage_n, i)))
                    r = inv[:, i % 4, :]
                    if j.get("keys", S) != S:
                        do(dve.tensor_scalar(total[:, i % 4, :], total[:, i % 4, :], 1e-30, None, ALU.add))
                    do(dve.reciprocal(r, total[:, i % 4, :]))
                    if "gate" in j:
                        do(dve.tensor_tensor(r, r, gate_t[:, :, j["gate"]], ALU.mult))
                    b, n = bank(lane, "x")
                    dve.wait_ge(*lane.of(("full", "x", n)))
                    dst = named[j["out"][0]]
                    at = j["out"][1]
                    for t in range(T):
                        o = dst[:, t, at:at + dv] if j["out"][0] != "DO" else DO[:, t, at:at + dv]
                        if j.get("add"):
                            ins = dve.scalar_tensor_tensor(o, b[:, t * dv:(t + 1) * dv], r[:, t:t + 1], o,
                                                           ALU.mult, ALU.add)
                        else:
                            ins = dve.tensor_scalar(o, b[:, t * dv:(t + 1) * dv], r[:, t:t + 1], None, ALU.mult)
                        if t < T - 1:
                            post(ins)
                        else:
                            post(ins, ("free", "x", n), ("normed", stage_n, i), sem=x_free)

                for i in range(count + 4):
                    if 0 <= i - 1 < count:
                        scores(i - 1)
                    if 0 <= i - 4 < count:
                        normed(i - 4)

            def diff_out(s, stage_n):
                l = s["l"]
                init = 0.8 - 0.6 * math.exp(-0.3 * l)
                lam = small[:, SV_LAM:SV_LAM + 128].rearrange("p (a b c) -> p a b c", a=2, b=2)
                for m in range(2):
                    do(dve.tensor_tensor_reduce(PR[:, 0, 0, 0:32], lam[:, m, 0, :], lam[:, m, 1, :], 1.0, 0.0,
                                                ALU.mult, ALU.add, stat[:, m:m + 1]), ("lambda", l))
                dve.wait_ge(*lane.of(("lambda_exp", l)))
                do(dve.tensor_tensor(stat[:, 60:61], stat[:, 1:2], stat[:, 0:1], ALU.subtract))
                do(dve.tensor_scalar(stat[:, 60:61], stat[:, 60:61], -init, None, ALU.add))
                for t in range(T):
                    o = DO[:, t, 0:256]
                    do(dve.scalar_tensor_tensor(o, DO[:, t, 256:512], stat[:, 60:61], o, ALU.mult, ALU.add))
                    do(dve.tensor_tensor(PR[:, 0, t, 0:256], o, o, ALU.mult))
                    do(dve.tensor_reduce(stat[:, 32 + 4 * t:36 + 4 * t],
                                         PR[:, 0, t, 0:256].rearrange("p (h c) -> p h c", h=4), AX, ALU.add))
                inv_root(8, stat[:, 32:40], 1.0 / HD, EPS)
                do(dve.tensor_scalar(small[:, SV_SUB:SV_SUB + HD], small[:, SV_SUB:SV_SUB + HD], 1.0 - init, None,
                                     ALU.mult))
                for t in range(T):
                    o = DO[:, t, 0:256].rearrange("p (h c) -> p h c", h=4)
                    do(dve.tensor_tensor(o, o, stat[:, 4 * t:4 * t + 4].unsqueeze(2).broadcast_to([P, 4, HD]), ALU.mult))
                    do(dve.tensor_tensor(O[:, t, 256:512].rearrange("p (h c) -> p h c", h=4), o,
                                         small[:, SV_SUB:SV_SUB + HD].unsqueeze(1).broadcast_to([P, 4, HD]),
                                         ALU.mult), ("diff", l))

            def select(s):
                dve.wait_ge(*lane.of(("bias", s["bias"])))
                do(dve.tensor_tensor(score, score, bias_t[:, s["bias"] % BIAS_SLOTS], ALU.add),
                   ("bias_used", s["bias"]))
                ones = SC[:, 1, 0, 0:S]
                do(dve.memset(ones, 1.0))
                for t in range(T):
                    do(dve.tensor_copy(work[:, t, :], score[:, t, :]))
                    for r in range(TOPK // 8):
                        do(dve.max(stat[:, 8:16], work[:, t, :]))
                        if r < TOPK // 8 - 1:
                            do(dve.match_replace(work[:, t, :], stat[:, 8:16], work[:, t, :], -3e38))
                    above, equal, order = SC[:, 0, 0, 0:S], SC[:, 0, 1, 0:S], PR[:, 0, 0, 0:S]
                    do(dve.tensor_scalar(above, score[:, t, :], stat[:, 15:16], 0.0, ALU.is_gt, ALU.add,
                                         accum_out=stat[:, 16:17]))
                    do(dve.tensor_scalar(stat[:, 17:18], stat[:, 16:17], -1.0, float(TOPK), ALU.mult, ALU.add))
                    do(dve.tensor_scalar(equal, score[:, t, :], stat[:, 15:16], None, ALU.is_equal))
                    do(dve.tensor_tensor_scan(order, ones, equal, 0.0, ALU.mult, ALU.add))
                    do(dve.scalar_tensor_tensor(order, order, stat[:, 17:18], equal, ALU.is_le, ALU.mult))
                    do(dve.tensor_tensor(order, order, above, ALU.add))
                    do(dve.tensor_scalar(score[:, t, :], order, -1.0, -NEG, ALU.add, ALU.mult))

            def compress(s):
                dve.wait_ge(*lane.of(("compress_turned", s["n"])))
                kt = QK[0:HD, 0, :, :].rearrange("p (g t) n -> p g (t n)", g=2)
                for g in range(2):
                    src = bass.AP(QK, kt[:, g, :].offset, [[kt.ap[0][0], HD], [1, 32], [16, CMP]])
                    do(dve.tensor_tensor(KPE[:, g], src, PET.unsqueeze(2).broadcast_to([HD, 32, CMP]), ALU.add),
                       ("blocks", s["n"]))
                b, n = bank(lane, "d")
                dve.wait_ge(*lane.of(("full", "d", n)))
                w = 2 * CMP
                x, u = GEL[:, 0, 0:w], GEL[:, 1, 0:w]
                do(dve.tensor_copy(x, b[:, 0:w]), ("free", "d", n), sem=d_free)
                do(dve.tensor_tensor(u, x, x, ALU.mult))
                do(dve.tensor_scalar(u, u, 0.044715, 1.0, ALU.mult, ALU.add))
                do(dve.tensor_tensor(GEL[:, 3, 0:w], u, x, ALU.mult), ("gelu_arg", s["n"]))
                dve.wait_ge(*lane.of(("gelu_exp", s["n"])))
                do(dve.tensor_scalar(u, GEL[:, 4, 0:w], 1.0, None, ALU.add))
                do(dve.reciprocal(u, u))
                do(dve.tensor_tensor(GEL[:, 5, 0:w], x, u, ALU.mult), ("gelu", s["n"]))

            def route_tokens():
                dve.wait_ge(*lane.of(("index",)))
                top = route[:, 0:16].rearrange("p (t e) -> p t e", t=T)
                where = route[:, 16:32].bitcast(U32).rearrange("p (t e) -> p t e", t=T)
                for t in range(T):
                    do(dve.max(top[:, t, :], logits[:, t, :]))
                    do(dve.max_index(where[:, t, :], top[:, t, :], logits[:, t, :]))
                    do(dve.tensor_tensor(route[:, 32 + t:33 + t], top[:, t, 1:2], top[:, t, 0:1], ALU.subtract),
                       ("route_arg",))
                dve.wait_ge(*lane.of(("route_exp",)))
                do(dve.tensor_scalar(route[:, 34:36], route[:, 32:34], 1.0, None, ALU.add))
                do(dve.reciprocal(route[:, 34:36], route[:, 34:36]))
                do(dve.tensor_tensor(route[:, 36:38], route[:, 32:34], route[:, 34:36], ALU.mult))
                do(dve.tensor_copy(route[:, 40:56].rearrange("p (t e) -> p t e", t=T), where))
                at = route[:, 40:56].rearrange("p (t e) -> p t e", t=T)
                for t in range(T):
                    do(dve.tensor_scalar(gate_t[:, t, 0:8], small[:, 0:8], at[:, t, 0:1], route[:, 34 + t:35 + t],
                                         ALU.is_equal, ALU.mult))
                    do(dve.tensor_scalar(route[:, 56:64], small[:, 0:8], at[:, t, 1:2], route[:, 36 + t:37 + t],
                                         ALU.is_equal, ALU.mult))
                    do(dve.tensor_tensor(gate_t[:, t, 0:8], gate_t[:, t, 0:8], route[:, 56:64], ALU.add))
                do(dve.memset(O[:, :, :], 0.0))

            def ffn(groups):
                for group in groups:
                    n_group = state["group"]
                    state["group"] += 1
                    dve.wait_ge(*lane.back(("down",), n_group - 2, book["group_first"], book["group_body"]))
                    for f0 in range(0, group["w"] // P, 2):
                        p = state["pair"]
                        state["pair"] += 1
                        dve.wait_ge(*lane.of(("silu", p)))
                        b, n = bank(lane, "d")
                        dve.wait_ge(*lane.of(("full", "d", n)))
                        dve.tensor_tensor(
                            hid[:, n_group % 2, f0:f0 + 2, :].rearrange("p f s -> p (f s)"), silu[:, p % 2, :],
                            b[:, :], ALU.mult).then_inc(*lane.tick(d_free, ("free", "d", n), ("hidden", p)))

            for n, (kind, s) in enumerate(stages):
                if kind not in ("turn", "linear", "load_x", "load_mem", "small", "lines"):
                    dve.wait_ge(*lane.of(("done", "tensor", n - 1)))
                    dve.wait_ge(*lane.of(("done", "scalar", n - 1)))
                    dve.wait_ge(*lane.of(("done", "gpsimd", n - 1)))
                if kind == "lines":
                    dve.wait_ge(*lane.of(("x",)))
                    b, m = bank(lane, "d")
                    dve.wait_ge(*lane.of(("full", "d", m)))
                    for v in range(2):
                        do(dve.tensor_tensor(lines[:, v, :], b[0:16, :], line_mask[:, v, :], ALU.add),
                           ("lines",), ("free", "d", m), sem=d_free)
                    dve.wait_ge(*lane.of(("const",)))
                    dve.wait_ge(*lane.of(("line_stored",)))
                    dve.wait_ge(*lane.of(("table_stored", DEPTH - 1)))
                elif kind == "rms_pre":
                    rms_pre(s)
                elif kind == "rms_add":
                    rms_add(s)
                elif kind == "layer_norm":
                    layer_norm(s)
                elif kind == "head_norms":
                    head_norms(s)
                elif kind == "mla_keys":
                    mla_keys()
                elif kind == "attend":
                    attend(s, n)
                elif kind == "diff_out":
                    diff_out(s, n)
                elif kind == "latent_norm":
                    dve.wait_ge(*lane.of(("latent",)))
                    c = proj[:, :, 512:640]
                    squares(c, P, PR[:, 0, :, :])
                    inv_root(T, stat[:, 32:34], 1.0 / P, LN_EPS)
                    for t in range(T):
                        do(dve.scalar_tensor_tensor(c[:, t, :], c[:, t, :], stat[:, t:t + 1], small[:, 0:P],
                                                    ALU.mult, ALU.mult))
                    do(dve.tensor_scalar(proj[:, :, 1216:1224], proj[:, :, 1216:1224], 8 ** -0.5, None, ALU.mult))
                elif kind == "index_scores":
                    do(dve.memset(score, 0.0))
                    for h in range(8):
                        dve.wait_ge(*lane.of(("relu", h)))
                        for t in range(T):
                            do(dve.scalar_tensor_tensor(score[:, t, :], SC[:, h % 2, t, 0:S],
                                                        proj[:, t, 1216 + h:1217 + h], score[:, t, :],
                                                        ALU.mult, ALU.add), ("indexed", h))
                elif kind == "select":
                    select(s)
                elif kind == "gates":
                    dve.wait_ge(*lane.of(("gate_exp",)))
                    do(dve.tensor_scalar(gate_t[:, :, :], gate_t[:, :, :], 1.0, None, ALU.add))
                    do(dve.reciprocal(gate_t[:, :, :], gate_t[:, :, :]))
                elif kind == "compress":
                    compress(s)
                elif kind == "route":
                    route_tokens()
                elif kind == "ffn":
                    ffn(s["groups"])
                    for t in range(T):
                        for half in range(2):
                            b, m = bank(lane, "x")
                            dve.wait_ge(*lane.of(("full", "x", m)))
                            dve.tensor_copy(N[:, t, 512 * half:512 * half + 512], b[:, :]).then_inc(*lane.tick(x_free, ("free", "x", m)))
                    dve.wait_ge(*lane.own())
                elif kind == "experts":
                    book["group_first_new"] = state["group"]
                    with lane.loop(dve, EXPERTS // BODY) as turn:
                        for u, groups in enumerate(s["groups"]):
                            ffn(groups)
                            for t in range(T):
                                for half in range(2):
                                    b, m = bank(lane, "x")
                                    dve.wait_ge(*lane.of(("full", "x", m)))
                                    y = O[:, t, 512 * half:512 * half + 512]
                                    dve.scalar_tensor_tensor(
                                        y, b[:, :], gate_t[:, t, bass.ds(turn * BODY + u, 1)], y,
                                        ALU.mult, ALU.add).then_inc(*lane.tick(x_free, ("free", "x", m)))
                    book["group_body_new"] = state["group"] - book["group_first_new"]
                    dve.wait_ge(*lane.own())
                    do(dve.tensor_copy(N[:, :, :], O[:, :, :]))
                leave(lane, n)


def new_book(old=None):
    old = old or {}
    return {"first": not old, "known": old.get("new", {}), "new": {}, "step": old.get("step_new", {}), "step_new": {},
            "turns": EXPERTS // BODY, "ring_first": old.get("ring_first_new", {}), "ring_first_new": {},
            "ring_body": old.get("ring_body_new", {}), "ring_body_new": {}, "width": old.get("width", {}),
            "pair_first": old.get("pair_first_new", 0), "pair_body": old.get("pair_body_new", 0),
            "group_first": old.get("group_first_new", 0), "group_body": old.get("group_body_new", 0)}


def kernel(**inputs):
    import numpy as _np
    import concourse.bacc as _bacc
    from concourse import mybir as _mybir
    from concourse.bass_utils import run_bass_kernel_spmd as _run

    host = {k: _np.ascontiguousarray(v) for k, v in inputs.items()}
    host.update(shape_constants())
    book = None
    for _ in range(2):
        book = new_book(book)
        nc = _bacc.Bacc("TRN2", target_bir_lowering=False, num_devices=1)
        a = {k: nc.dram_tensor(f"in_{k}", v.shape, _mybir.dt.from_np(v.dtype), kind="ExternalInput").ap()
             for k, v in host.items()}
        out = nc.dram_tensor("out_0", (1, S, D), F32, kind="ExternalOutput").ap()
        build(nc, a, out, book)
    r = _run(nc, [{f"in_{k}": v for k, v in host.items()}], core_ids=[0])
    return r.results[0]["out_0"]
```

```python
import math
from contextlib import ExitStack, contextmanager

import numpy as np

import concourse.bass as bass
from concourse import mybir

F32 = mybir.dt.float32
U32 = mybir.dt.uint32
I32 = mybir.dt.int32
ALU = mybir.AluOpType
ACT = mybir.ActivationFunctionType
AX = mybir.AxisListType.X

P = 128
D = 1024
S = 256
T = S // P
KD = D // P
DEPTH = 2
GRID_W = 64
ROWS = S // GRID_W
NA_ROWS, NA_COLS = 8, 16
HD = 64
EPS, LN_EPS = 1e-6, 1e-5
ALPHA = (2 * DEPTH) ** 0.25
NEG = -1e30
IN_W = 2464
EV_W = 1992
OD_W = 1840
D_FF = 2816
D_EXP = 3584
EXPERTS = 8
TOPK = 64
CMP = 15
SLOT = 4096
SLOTS = 6
RINGS = {"a": 2, "d": 2, "x": 4}
BODY = 2
LOOP_TURNS = EXPERTS // BODY
BIAS_SLOTS = 3
VEC_SLOTS = 3
NEAR = 2 * ROWS - 1
ROPE_THETA = 10000.0

NA_Q, NA_K, NA_V, DF_Q, DF_K, DF_V = 0, 256, 512, 768, 1024, 1280
GQ_Q, GQ_K, GQ_V, ML_Q, ML_KV, ML_KR = 1536, 1792, 1920, 2048, 2304, 2432
SV_GQ, SV_GK, SV_MQ, SV_MKV, SV_SUB, SV_LAM, SV_END = 0, 64, 128, 384, 512, 576, 704


def shape_constants():
    f = np.float32
    pos = np.arange(S)
    inv = (f(ROPE_THETA) ** (-np.arange(0, 32, 2, dtype=f) / f(32))).astype(f)
    rope = np.zeros((S, 3, 2, 16), f)
    for n, where in enumerate((pos // GRID_W, pos % GRID_W, pos)):
        angle = (where.astype(f)[:, None] * inv[None, :]).astype(f)
        rope[:, n, 0], rope[:, n, 1] = np.cos(angle), np.sin(angle)
    c = np.arange(GRID_W)
    start = np.clip(c - NA_COLS // 2, 0, GRID_W - NA_COLS)
    window = np.where((c[None] >= start[:, None]) & (c[None] < start[:, None] + NA_COLS), f(0), f(NEG))
    window = np.tile(window, (P // GRID_W, ROWS)).astype(f)
    dist = 255 - np.arange(512)
    apart = pos[:, None] - pos[None]
    alibi = np.stack([-f(2.0 ** (-8.0 * (h + 1) / 4)) * np.abs(apart).astype(f) for h in range(4)])
    after = np.where(apart >= 0, f(0), f(NEG))
    n = np.maximum(dist, 0)
    nf = np.maximum(n, 1).astype(f)
    log_b = 16 + (np.log(nf / f(16)) / f(math.log(8)) * f(16)).astype(np.int32)
    bucket = np.where(n < 16, n, np.minimum(log_b, 31))
    onehot = (np.arange(32)[:, None] == bucket[None]).astype(f)
    causal = np.where(dist >= 0, f(0), f(NEG))
    band = np.where((dist >= 0) & (dist < 128), f(0), f(NEG))
    return {
        "c_ident": np.eye(P, dtype=f), "c_rope": rope, "c_window": window, "c_alibi": alibi.astype(f),
        "c_bucket": onehot, "c_line": np.stack([causal, band]).astype(f),
        "c_index": np.arange(8, dtype=f)[None],
        "c_causal": after.astype(f), "c_slot": np.arange(P, dtype=f)[None],
        "c_earlier": np.triu(np.ones((P, P), f), 1),
    }


class Lane:

    def __init__(self, book, name, landed):
        self.book, self.name, self.landed = book, name, landed
        self.count, self.last = {}, None
        self.turn = None
        self.ring = {r: 0 for r in RINGS}

    def tick(self, sem, *keys, by=1):
        self.count[sem.name] = self.count.get(sem.name, 0) + by
        self.last = (sem, self.count[sem.name])
        self.mark(*keys)
        return sem, by

    def mark(self, *keys):
        if self.last:
            for key in keys:
                loop = self.turn and self.turn[0]
                self.book["new"][key] = (*self.last, loop)
                if loop:
                    span = self.book["span_new"].setdefault((loop, key[:-1]), [key[-1], key[-1]])
                    span[1] = key[-1]

    def of(self, key, before=False):
        known = self.book["known"].get(key)
        if known is None:
            assert self.book["first"] or key[0] == "done", key
            return self.landed, 16
        name, value, loop = known[0].name, known[1], known[2]
        sem = self.book["sems"][name]
        step = self.book["step"].get((loop, name), 0)
        if self.turn and self.turn[0] == loop:
            value = value - (step if before else 0)
            assert value > 0, key
            return sem, self.turn[1] * step + value
        return sem, value + step * (LOOP_TURNS - 1)

    def own(self):
        sem, value = self.last or (self.landed, 16)
        if self.turn:
            return sem, self.turn[1] * self.book["step"].get((self.turn[0], sem.name), 0) + value
        return sem, value

    def back(self, what, n):
        if n < 0:
            return self.landed, 16
        if self.turn:
            first, last = self.book["span"].get((self.turn[0], what), (0, 0))
            if n < first:
                return self.of((*what, n + last + 1 - first), before=True)
        return self.of((*what, n))

    @contextmanager
    def loop(self, eng, name):
        start = dict(self.count)
        with eng.Fori(0, LOOP_TURNS) as turn:
            self.turn = (name, turn)
            yield turn
            self.turn = None
        for sem, value in self.count.items():
            step = value - start.get(sem, 0)
            if step:
                self.book["step_new"][name, sem] = step
                self.count[sem] = value + step * (LOOP_TURNS - 1)
        self.last = (self.last[0], self.count[self.last[0].name])

    def since(self, start):
        return [(self.book["sems"][sem], value - start.get(sem, 0)) for sem, value in self.count.items()
                if value > start.get(sem, 0)]


def plan(a):
    stages, blocks, biases, vectors = [], [], [], []

    def block(src, p, k, c):
        blocks.append((src, p, k, c))
        return len(blocks) - 1

    def columns(w, width, k=KD):
        view = w.rearrange("(k p) c -> p k c", p=P)
        out = []
        for c0 in range(0, width, 512):
            c = min(512, width - c0)
            out.append((block(view[:, :, c0:c0 + c], P, k, c), c0, c))
        return out

    def vector(src):
        vectors.append(src)
        return len(vectors) - 1

    def bias(*what):
        biases.append(what)
        return len(biases) - 1

    def stage(kind, **args):
        stages.append((kind, args))

    def ffn(gate, up, down, width):
        gv, uv = (w.rearrange("(k p) c -> p k c", p=P) for w in (gate, up))
        widths = [min(512, width - c0) for c0 in range(0, width, 512)]
        groups, late = [], None
        for g, w in enumerate(widths):
            c0 = 512 * g
            gb = block(gv[:, :, c0:c0 + w], P, KD, w)
            ub = block(uv[:, :, c0:c0 + w], P, KD, w)
            if late is not None:
                groups[-1]["down"] = block(late, P, groups[-1]["w"] // P, D)
            late = down[c0:c0 + w, :].rearrange("(k p) c -> p k c", p=P)
            groups.append({"gate": gb, "up": ub, "w": w})
        groups[-1]["down"] = block(late, P, widths[-1] // P, D)
        return groups

    stage("load_x")
    stage("lines")
    for l in range(DEPTH):
        stage("small", l=l)
        stage("rms_pre", vec=vector(a["pre_mix_norm"][l]))
        stage("turn", src="N", dst="hT", chunks=KD)
        stage("linear", lhs="hT", k=KD, blocks=columns(a["w_in"][l], IN_W), dst="proj")
        stage("head_norms", l=l)
        stage("turn", src="mla_lat", dst="hT", chunks=3)
        uq = block(a["mla_w_uq"][l].rearrange("(k p) c -> p k c", p=P), P, 2, 384)
        ukv = block(a["mla_w_ukv"][l].rearrange("(k p) c -> p k c", p=P), P, 1, 512)
        stage("linear", lhs="hT", k=2, blocks=[(uq, 0, 384)], dst="QF")
        stage("linear", lhs="hT2", k=1, blocks=[(ukv, 0, 512)], dst="KV")
        stage("mla_keys", l=l)
        jobs = []
        for h in range(4):
            jobs.append(dict(q=("proj", NA_Q + HD * h), k=("proj", NA_K + HD * h), v=("proj", NA_V + HD * h), d=HD,
                             dv=HD, scale=HD ** -0.5, bias=bias("na", l, h), out=("O", HD * h)))
        for h in range(4):
            b = bias("alibi", h)
            for j in range(2):
                o = 64 * h + 32 * j
                jobs.append(dict(q=("proj", DF_Q + o), k=("proj", DF_K + o), v=("proj", DF_V + HD * h), d=32,
                                 dv=HD, scale=32 ** -0.5, bias=b, out=("DO", 256 * j + HD * h)))
        for h in range(4):
            jobs.append(dict(q=("proj", GQ_Q + HD * h), k=("proj", GQ_K + HD * (h // 2)),
                             v=("proj", GQ_V + HD * (h // 2)), d=HD, dv=HD, scale=HD ** -0.5, bias=None,
                             out=("O", 512 + HD * h)))
        for h in range(4):
            jobs.append(dict(q=("QF", 96 * h), k=("KF", 96 * h), v=("KV", 128 * h + 64), d=96, dv=HD,
                             scale=96 ** -0.5, bias=None, out=("O", 768 + HD * h)))
        stage("attend", jobs=jobs)
        stage("diff_out", l=l)
        stage("turn", src="O", dst="hT", chunks=KD)
        stage("linear", lhs="hT", k=KD, blocks=columns(a["w_o"][l], D), dst="N")
        stage("rms_add", vec=vector(a["post_mix_norm"][l]))
        stage("rms_pre", vec=vector(a["pre_ffn_norm"][l]))
        stage("turn", src="N", dst="hT", chunks=KD)
        gu = a["ffn_w_gate_up"][l]
        stage("ffn", groups=ffn(gu[:, 0:D_FF], gu[:, D_FF:2 * D_FF], a["ffn_w_down"][l], D_FF))
        stage("rms_add", vec=vector(a["post_ffn_norm"][l]))

    def cross(i):
        stage("turn", src="X", dst="hT", chunks=KD)
        stage("linear", lhs="hT", k=KD, blocks=columns(a["xa_w_q_2"][i], 512), dst="proj")
        stage("linear", lhs="memT", k=KD, blocks=columns(a["xa_w_k_2"][i], 512), dst="proj@512")
        stage("linear", lhs="memT", k=KD, blocks=columns(a["xa_w_v_2"][i], 512), dst="proj@1024")
        stage("attend", jobs=[dict(q=("proj", P * h), k=("proj", 512 + P * h), v=("proj", 1024 + P * h), d=P, dv=P,
                                   scale=P ** -0.5, bias=None, out=("O", P * h)) for h in range(4)])
        stage("turn", src="O", dst="hT", chunks=4)
        wo = block(a["xa_w_o_2"][i].rearrange("(k p) c -> p k c", p=P), P, 4, D)
        stage("linear", lhs="hT", k=4, blocks=[(wo, 0, D)], dst="N")
        norm(i, 1)

    def norm(i, j):
        stage("layer_norm", gain=vector(a["ln_g_2"][i, j]), shift=vector(a["ln_b_2"][i, j]))

    stage("load_mem")
    stage("turn", src="N", dst="memT", chunks=KD)
    stage("turn", src="X", dst="hT", chunks=KD)
    stage("linear", lhs="hT", k=KD, blocks=columns(a["ev_w_in_2"][0], EV_W), dst="proj")
    stage("latent_norm")
    stage("index_scores")
    stage("select", bias=bias("line", "causal"))
    uk = block(a["ev_w_uk_2"][0].rearrange("h d c -> d h c"), HD, 8, P)
    uv = block(a["ev_w_uv_2"][0].rearrange("h c d -> c h d"), P, 8, HD)
    stage("latent_heads", uk=uk, uv=uv)
    jobs = []
    for h in range(8):
        g = h // 4
        jobs.append(dict(q=("proj", 1224 + HD * h), k=("proj", 1736 + HD * g), v=("proj", 1864 + HD * g), d=HD, dv=HD,
                         scale=HD ** -0.5, bias=bias("band", h + 8), sink=h, out=("O", 512 + HD * h)))
    for h in range(8):
        jobs.append(dict(qT=("QL", h), kT="cT", v=("VC", HD * h), d=P, dv=HD, scale=HD ** -0.5,
                         bias=bias("causal", h), selected=True, out=("O", HD * h)))
    stage("attend", jobs=jobs)
    stage("turn", src="O", dst="hT", chunks=KD)
    stage("linear", lhs="hT", k=KD, blocks=columns(a["ev_w_out_2"][0], D), dst="N")
    norm(0, 0)
    cross(0)
    stage("turn", src="X", dst="hT", chunks=KD)
    stage("ffn", groups=ffn(a["ff_w_gate_2"][0], a["ff_w_up_2"][0], a["ff_w_down_2"][0], D_FF))
    norm(0, 2)
    stage("turn", src="X", dst="hT", chunks=KD)
    stage("linear", lhs="hT", k=KD, blocks=columns(a["od_w_in_2"][0], OD_W), dst="proj")
    stage("gates")
    for n, x in enumerate("kv"):
        w1 = block(a[f"od_w1_{x}_2"][0].rearrange("(i d) c -> d i c", d=HD), HD, 32, P)
        w2 = block(a[f"od_w2_{x}_2"][0].rearrange("(k p) c -> p k c", p=P), P, 1, HD)
        stage("compress", n=n, w1=w1, w2=w2)
    jobs = []
    for h in range(16):
        g = h // 8
        b = bias("causal", h)
        q = ("proj", HD * h)
        common = dict(q=q, d=HD, dv=HD, scale=HD ** -0.5, bias=b, out=("O", HD * h))
        jobs.append(dict(common, kT=("KC", g), v=("VCMP", g), keys=CMP, gate=3 * h))
        jobs.append(dict(common, k=("proj", 1280 + HD * g), v=("proj", 1408 + HD * g), gate=3 * h + 1, add=True))
        jobs.append(dict(common, k=("proj", 1536 + HD * g), v=("proj", 1664 + HD * g), gate=3 * h + 2, add=True))
    stage("attend", jobs=jobs)
    stage("turn", src="O", dst="hT", chunks=KD)
    stage("linear", lhs="hT", k=KD, blocks=columns(a["od_w_out_2"][0], D), dst="N")
    norm(1, 0)
    cross(1)
    stage("turn", src="X", dst="hT", chunks=KD)
    stage("linear", lhs="hT", k=KD, blocks=columns(a["moe_w_router_2"][0], EXPERTS), dst="logits")
    stage("route")
    for tile in range(T):
        first = len(blocks)
        groups = [ffn(a["moe_w_gate_2"][0, u], a["moe_w_up_2"][0, u], a["moe_w_down_2"][0, u], D_EXP)
                  for u in range(BODY)]
        stage("experts", groups=groups, first=first, tile=tile, count=len(blocks) - first)
    norm(1, 2)
    stage("store_x")
    for kind, args in stages:
        if kind == "attend":
            last = {}
            for n, j in enumerate(args["jobs"]):
                last[j["bias"]] = n
            for n, j in enumerate(args["jobs"]):
                j["bias_last"] = last[j["bias"]] == n
    return stages, blocks, biases, vectors


def build(nc, a, out, book, cut=None):
    stages, blocks, biases, vectors = plan(a)
    if cut is not None:
        stages = stages[:cut] + [("store_x", {})]
    expert_stages = [s for kind, s in stages if kind == "experts"]
    used_blocks = {b[0] for _, s in stages for b in s.get("blocks", [])}
    for _, s in stages:
        for g in s.get("groups", []):
            for x in (g if isinstance(g, list) else [g]):
                used_blocks |= {x["gate"], x["up"], x["down"]}
        used_blocks |= {s[k] for k in ("uk", "uv", "w1", "w2") if k in s}
    blocks = blocks[:max(used_blocks | {-1}) + 1]
    used_bias = {s["bias"] for _, s in stages if "bias" in s} | {j["bias"] for _, s in stages for j in s.get("jobs", [])}
    biases = biases[:max([b for b in used_bias if b is not None], default=-1) + 1]
    vectors = vectors[:max([s[k] for _, s in stages for k in ("vec", "gain", "shift") if k in s], default=-1) + 1]

    with ExitStack() as ctx:
        def sb(name, shape, dt=F32):
            return ctx.enter_context(nc.sbuf_tensor(name, shape, dt))

        ps = {(r, n): ctx.enter_context(nc.psum_tensor(f"ps_{r}{n}", [P, 512], F32))
              for r, size in RINGS.items() for n in range(size)}
        book["sems"] = {}

        def sem(name):
            book["sems"][name] = ctx.enter_context(nc.semaphore(name))
            return book["sems"][name]

        a_full, a_free, d_full, d_free, x_full, x_free = (
            sem(n) for n in ("a_full", "a_free", "d_full", "d_free", "x_full", "x_free"))
        filled = {"a": a_full, "d": d_full, "x": x_full}
        down_done = sem("down_done")
        slot_landed = [sem(f"slot_landed{n}") for n in range(SLOTS)]
        bias_landed = [sem(f"bias_landed{n}") for n in range(BIAS_SLOTS)]
        vec_landed = [sem(f"vec_landed{n}") for n in range(VEC_SLOTS)]
        x_landed, mem_landed, const_landed, small_landed, gain_landed, pe_landed = (
            sem(n) for n in ("x_landed", "mem_landed", "const_landed", "small_landed", "gain_landed", "pe_landed"))
        table_loaded, table_stored, line_stored, stored = (
            sem(n) for n in ("table_loaded", "table_stored", "line_stored", "stored"))
        dve_order, act_order, pool_order, exped, maxed = (
            sem(n) for n in ("dve_order", "act_order", "pool_order", "exped", "maxed"))

        slots = sb("slots", [P, SLOTS, SLOT])
        X = sb("X", [P, T, D])
        N = sb("N", [P, T, D])
        hT = sb("hT", [P, KD, S])
        mid = sb("mid", [P, 2560])
        proj = sb("proj", [P, T, IN_W])
        O = sb("O", [P, T, D])
        DO = sb("DO", [P, T, 512])
        bias_t = sb("bias_t", [P, BIAS_SLOTS, T, S])
        SC = sb("SC", [P, 2, T, S + 1])
        PR = sb("PR", [P, 2, T, S + 1])
        PT = sb("PT", [P, 2, 2, T, P])
        QK = sb("QK", [P, 2, 4, P])
        vec = sb("vec", [P, VEC_SLOTS, D])
        small = sb("small", [P, SV_END])
        ident = sb("ident", [P, P])
        rope_t = sb("rope_t", [P, T, 3, 2, 16])
        window = sb("window", [P, S])
        negmax = sb("negmax", [P, 4, T])
        total = sb("total", [P, 4, T])
        inv = sb("inv", [P, 4, T])
        stat = sb("stat", [P, 64])
        gate_t = sb("gate_t", [P, T, 48])

        QF = mid[:, 0:768].rearrange("p (t c) -> p t c", t=T)
        KV = mid[:, 768:1792].rearrange("p (t c) -> p t c", t=T)
        KF = mid[:, 1792:2560].rearrange("p (t c) -> p t c", t=T)
        memT = mid[:, 0:2048].rearrange("p (k s) -> p k s", k=KD)
        flat = proj[:, :, :].rearrange("p t c -> p (t c)")
        hid = flat[:, 0:2048].rearrange("p (b f s) -> p b f s", b=2, f=4)
        hid_e = flat[:, 0:1024].rearrange("p (b f s) -> p b f s", b=2, f=4)
        silu_e = flat[:, 1024:2048].rearrange("p (b s) -> p b s", b=2)
        pick = flat[:, 2048:2560].rearrange("p (b t s) -> p b t s", b=2, t=T)
        weigh = flat[:, 2560:3072].rearrange("p (b t s) -> p b t s", b=2, t=T)
        give = flat[:, 3200:3712].rearrange("p (b s) -> p b s", b=2)
        y_e = flat[:, 3712:4736]
        xg = hT[:, :, :].rearrange("p k s -> p (k s)").rearrange("p (b k s) -> p b k s", b=2, k=KD)
        slot_row = window[:, 0:P]
        place = small[:, 16:32].rearrange("p (t e) -> p t e", t=T)
        chosen = small[:, 32:48].rearrange("p (t e) -> p t e", t=T)
        load_f = small[:, 48:56]
        loads = sb("loads", [P, EXPERTS], I32)
        earlier, every = QK[:, 0, 0, :], QK[:, 0, 1, :]
        silu = flat[:, 2048:3072].rearrange("p (b s) -> p b s", b=2)
        logits = flat[:, 3072:3088].rearrange("p (t e) -> p t e", t=T)
        route = flat[:, 3088:3200]
        NF = N[:, :, :].rearrange("p t c -> p (t c)")
        VC = NF[:, 0:1024].rearrange("p (t c) -> p t c", t=T)
        score = NF[:, 1024:1536].rearrange("p (t s) -> p t s", t=T)
        work = NF[:, 1536:2048].rearrange("p (t s) -> p t s", t=T)
        cT = DO[:, 0, 0:S]
        KC = DO[0:HD, 0, 0:2 * CMP].rearrange("p (g n) -> p g n", g=2)
        VCMP = DO[0:CMP, 0, 32:160].rearrange("p (g n) -> p g n", g=2)
        GEL = DO[:, 0, 160:160 + 6 * 32].rearrange("p (a n) -> p a n", a=6)
        PET = DO[0:HD, 0, 352:384]
        PEN = DO[0:32, 0, 384:384 + HD]
        KPE = NF[0:HD, 0:2 * 32 * CMP].rearrange("p (g i n) -> p g i n", g=2, i=32)
        onehot = flat[0:32, 0:512]
        table = flat[0:32, 512:528]
        line_mask = flat[0:16, 1024:2048].rearrange("p (a n) -> p a n", a=2)
        lines = flat[0:16, 2048:3072].rearrange("p (a n) -> p a n", a=2)
        padded = NF[0:4 * NEAR, 0:P]
        named = {"N": N, "X": X, "O": O, "proj": proj, "QF": QF, "KV": KV, "KF": KF, "DO": DO, "hT": hT,
                 "memT": memT, "VC": VC, "logits": logits, "proj@512": proj[:, :, 512:1024],
                 "proj@1024": proj[:, :, 1024:1536], "mla_lat": proj[:, :, ML_Q:ML_Q + 384],
                 "hT2": hT[:, 2:3, :]}

        line_d = nc.dram_tensor("line_scratch", (2, 16, P, 512), F32, kind="Internal").ap()
        table_d = nc.dram_tensor("table_scratch", (DEPTH, 4 * NEAR, GRID_W, P), F32, kind="Internal").ap()

        block = ctx.enter_context(nc.Block())
        def bank(lane, r):
            n = lane.ring[r]
            lane.ring[r] += 1
            return ps[r, n % RINGS[r]], n

        def emptied(lane, r, n):
            return lane.back(("free", r), n - RINGS[r])

        def leave(lane, n):
            lane.mark(("done", lane.name, n))

        def skewed(line, t):
            return bass.AP(line_d.tensor, line * P * 512 + 127 + P * (T - 1 - t), [[511, P], [1, S]])

        @block.sync
        def _(sp):
            lane = Lane(book, "sync", x_landed)
            sp.dma_start(X[:, :, :], a["x"][0].rearrange("(t p) c -> p t c", p=P)).then_inc(*lane.tick(x_landed, ("x",), by=16))

            def load(n, src):
                _, p, k, c = blocks[n]
                dst = slots[0:p, n % SLOTS, 0:k * c].rearrange("p (k c) -> p k c", k=k)
                with nc.allow_non_contiguous_dma(reason="narrow weights"):
                    sp.dma_start(dst, src).then_inc(*lane.tick(slot_landed[n % SLOTS], ("weights", n), by=16))

            for n in range(expert_stages[0]["first"] if expert_stages else len(blocks)):
                if n >= SLOTS:
                    sp.wait_ge(*lane.of(("used", n - SLOTS)))
                load(n, blocks[n][0])

            def expert(e, groups):
                gate, up, down = (w[0, bass.ds(e, 1)].rearrange("e (k p) c -> p (e k) c", p=P) for w in (
                    a["moe_w_gate_2"], a["moe_w_up_2"], a["moe_w_down_2"]))
                order = []
                for g, group in enumerate(groups):
                    c0 = 512 * g
                    order += [(group["gate"], gate[:, :, c0:c0 + 512]), (group["up"], up[:, :, c0:c0 + 512]),
                              (group["down"], down[:, 4 * g:4 * g + 4, :])]
                for n, src in sorted(order, key=lambda x: x[0]):
                    sp.wait_ge(*lane.back(("used",), n - SLOTS))
                    load(n, src)

            for s in expert_stages:
                for n in range(s["first"] - SLOTS, s["first"]):
                    sp.wait_ge(*lane.of(("used", n)))
                if s["tile"]:
                    sp.wait_ge(*lane.of(("loads", 0)))
                with lane.loop(sp, s["tile"] + 1) as turn:
                    for u, groups in enumerate(s["groups"]):
                        e = turn * BODY + u
                        if s["tile"] == 0:
                            expert(e, groups)
                            continue
                        start, before = dict(lane.count), lane.own()
                        n = sp.value_load(loads[0:1, bass.ds(e, 1)], min_val=0, max_val=S)
                        with sp.If(n > P * s["tile"]):
                            expert(e, groups)
                        with sp.Else():
                            added = {sem.name: count for sem, count in lane.since(start)}
                            for n in range(groups[0]["gate"] - SLOTS, groups[0]["gate"]):
                                landed = slot_landed[n % SLOTS]
                                sp.wait_ge(*lane.back(("weights",), n))
                                sp.sem_inc(landed, added[landed.name])
            sp.wait_ge(*lane.of(("done", "vector", len(stages) - 2)))
            sp.dma_start(out[0].rearrange("(t p) c -> p t c", p=P), X[:, :, :]).then_inc(*lane.tick(stored, ("stored",), by=16))
            sp.wait_ge(*lane.own())

        @block.gpsimd
        def _(pool):
            lane = Lane(book, "gpsimd", x_landed)
            with nc.allow_non_contiguous_dma(reason="small tables"):
                for dst, src in ((ident[:, :], a["c_ident"]), (window[:, :], a["c_window"]),
                                 (rope_t[:, :, :, :, :].rearrange("p t a b c -> p t (a b c)"),
                                  a["c_rope"].rearrange("(t p) a b c -> p t (a b c)", p=P)),
                                 (onehot, a["c_bucket"]), (table, a["rel_table_2"]),
                                 (line_mask, a["c_line"].unsqueeze(0).broadcast_to([16, 2, 512]))):
                    pool.dma_start(dst, src).then_inc(*lane.tick(const_landed, ("const",), by=16))
                for l in range(DEPTH):
                    if l:
                        pool.wait_ge(*lane.of(("table_stored", l - 1)))
                    pool.memset(padded, 0.0).then_inc(*lane.tick(pool_order))
                    pool.wait_ge(*lane.own())
                    for h in range(4):
                        pool.dma_start(padded[NEAR * h:NEAR * h + NEAR, 48:79],
                                                   a["na_rel_bias"][l, h, NA_ROWS - ROWS:NA_ROWS - ROWS + NEAR, :]).then_inc(*lane.tick(table_loaded, by=16))
                    pool.wait_ge(*lane.own())
                    pool.dma_start(table_d[l], padded.unsqueeze(1).broadcast_to([4 * NEAR, GRID_W, P])).then_inc(*lane.tick(table_stored, ("table_stored", l), by=16))
                pool.wait_ge(*lane.of(("table_stored", DEPTH - 1)))
                pool.wait_ge(*lane.of(("lines",)))
                for v, h0 in ((0, 0), (1, 8)):
                    pool.dma_start(line_d[v, h0:16], lines[h0:16, v, :].unsqueeze(1).broadcast_to(
                        [16 - h0, P, 512])).then_inc(*lane.tick(line_stored, ("line_stored",), by=16))

                todo = []
                for n, (kind, s) in enumerate(stages):
                    if kind == "small":
                        todo.append(("small", n, s["l"]))
                    if kind == "load_mem":
                        todo.append(("mem", n, None))
                    if kind == "latent_norm":
                        todo.append(("latent", n, None))
                    if kind == "compress":
                        todo.append(("pe", n, s["n"]))
                    for k in ("vec", "gain", "shift"):
                        if k in s:
                            todo.append(("vec", n, s[k]))
                    if kind == "select":
                        todo.append(("bias", n, s["bias"]))
                    if kind == "route":
                        todo.append(("index", n, None))
                    for b in sorted({j["bias"] for j in s.get("jobs", []) if j["bias"] is not None}):
                        todo.append(("bias", n, b))

                def spread(src):
                    return src.unsqueeze(0).broadcast_to([P, src.shape[0]])

                for what, n, m in todo:
                    if what == "small":
                        if m:
                            pool.wait_ge(*lane.of(("diff", m - 1)))
                        for at, src in ((SV_GQ, a["gqa_q_norm"]), (SV_GK, a["gqa_k_norm"]), (SV_MQ, a["mla_q_norm"]),
                                        (SV_MKV, a["mla_kv_norm"]), (SV_SUB, a["diff_subln"]),
                                        (SV_LAM, a["diff_lambda_q1"]), (SV_LAM + 32, a["diff_lambda_k1"]),
                                        (SV_LAM + 64, a["diff_lambda_q2"]), (SV_LAM + 96, a["diff_lambda_k2"])):
                            pool.dma_start(small[:, at:at + src.shape[1]], spread(src[m])).then_inc(*lane.tick(small_landed, ("small", m), by=16))
                    elif what == "mem":
                        pool.wait_ge(*lane.of(("done", "vector", n - 1)))
                        pool.dma_start(N[:, :, :], a["mem_2"][0].rearrange("(t p) c -> p t c", p=P)).then_inc(*lane.tick(mem_landed, ("mem",), by=16))
                    elif what == "latent":
                        pool.wait_ge(*lane.of(("diff", DEPTH - 1)))
                        pool.dma_start(small[:, 0:P], spread(a["ev_ckv_gain_2"][0])).then_inc(*lane.tick(gain_landed, ("latent",), by=16))
                        pool.dma_start(small[:, P:P + 8], spread(a["ev_sinks_2"][0])).then_inc(*lane.tick(gain_landed, ("latent",), by=16))
                    elif what == "index":
                        pool.wait_ge(*lane.of(("done", "vector", n - 2)))
                        pool.wait_ge(*lane.of(("done", "tensor", n - 2)))
                        for dst, src in ((small[:, 0:8], spread(a["c_index"][0])), (slot_row, spread(a["c_slot"][0])),
                                         (earlier, a["c_earlier"])):
                            pool.dma_start(dst, src).then_inc(*lane.tick(gain_landed, ("index",), by=16))
                    elif what == "pe":
                        pool.wait_ge(*lane.of(("done", "vector", n - 1)))
                        pool.wait_ge(*lane.of(("done", "tensor", n - 1)))
                        pool.dma_start(PEN, a["od_pe_k_2" if m == 0 else "od_pe_v_2"][0]).then_inc(*lane.tick(pe_landed, ("pe", m), by=16))
                    elif what == "vec":
                        if m >= VEC_SLOTS:
                            pool.wait_ge(*lane.of(("vec_used", m - VEC_SLOTS)))
                        pool.dma_start(vec[:, m % VEC_SLOTS, :], spread(vectors[m])).then_inc(*lane.tick(vec_landed[m % VEC_SLOTS], ("vec", m), by=16))
                    else:
                        kind, *where = biases[m]
                        landed = bias_landed[m % BIAS_SLOTS]
                        tile = bias_t[:, m % BIAS_SLOTS]
                        if m >= BIAS_SLOTS:
                            pool.wait_ge(*lane.of(("bias_used", m - BIAS_SLOTS)))
                        if kind == "na":
                            l, h = where
                            for t in range(T):
                                for half in range(P // GRID_W):
                                    row = T * t + half
                                    src = bass.AP(table_d.tensor,
                                                  ((l * 4 + h) * NEAR + ROWS - 1 - row) * GRID_W * P + GRID_W - 1,
                                                  [[P - 1, GRID_W], [GRID_W * P, ROWS], [1, GRID_W]])
                                    dst = tile[GRID_W * half:GRID_W * half + GRID_W, t, :].rearrange(
                                        "p (r c) -> p r c", r=ROWS)
                                    pool.dma_start(dst, src).then_inc(*lane.tick(landed, by=16))
                            pool.wait_ge(*lane.own())
                            pool.tensor_tensor(
                                tile, tile, window[:, :].unsqueeze(1).broadcast_to([P, T, S]), ALU.add).then_inc(*lane.tick(pool_order, ("bias", m)))
                        elif kind in ("alibi", "line"):
                            src = a["c_alibi"][where[0]] if kind == "alibi" else a["c_causal"]
                            pool.dma_start(tile, src.rearrange("(t p) k -> p t k", p=P)).then_inc(*lane.tick(landed, ("bias", m), by=16))
                        else:
                            pool.wait_ge(*lane.of(("line_stored",)))
                            for t in range(T):
                                pool.dma_start(tile[:, t, :], skewed(
                                    16 * (kind == "band") + where[0], t)).then_inc(*lane.tick(landed, ("bias", m), by=16))

        @block.tensor
        def _(pe):
            lane = Lane(book, "tensor", x_landed)
            state = {"group": 0, "pair": 0, "pass": 0, "e_group": 0}

            def slot(n):
                pe.wait_ge(*lane.of(("weights", n)))
                _, p, k, c = blocks[n]
                return slots[0:p, n % SLOTS, 0:k * c].rearrange("p (k c) -> p k c", k=k)

            def turn(s):
                src, dst = named[s["src"]], s["chunks"]
                for k0 in range(0, dst, 2):
                    b, n = bank(lane, "a")
                    pe.wait_ge(*emptied(lane, "a", n))
                    ks = range(k0, min(k0 + 2, dst))
                    for k in ks:
                        for t in range(T):
                            o = ((k - k0) * T + t) * P
                            last = pe.transpose(b[:, o:o + P], src[:, t, k * P:(k + 1) * P], ident[:, :])
                    last.then_inc(*lane.tick(a_full, ("full", "a", n)))

            def linear(s):
                lhs = named[s["lhs"]]
                for w, _, c in s["blocks"]:
                    v = slot(w)
                    for t in range(T):
                        for j in range(0, c, 512):
                            b, n = bank(lane, "a")
                            pe.wait_ge(*emptied(lane, "a", n))
                            width = min(512, c - j)
                            for k in range(s["k"]):
                                last = pe.matmul(b[:, 0:width], lhs[:, k, t * P:(t + 1) * P], v[:, k, j:j + width],
                                                 start=(k == 0), stop=(k == s["k"] - 1))
                            last.then_inc(*lane.tick(a_full, ("full", "a", n), ("used", w)))

            def attend(s, stage_n):
                jobs = s["jobs"]
                count = len(jobs)

                def heads(i):
                    j = jobs[i]
                    if "q" not in j:
                        return
                    b, n = bank(lane, "a")
                    pe.wait_ge(*emptied(lane, "a", n))
                    parts = [j["q"]] + ([j["k"]] if "k" in j else [])
                    for m, (name, c) in enumerate(parts):
                        for t in range(T):
                            last = pe.transpose(b[0:j["d"], (m * T + t) * P:(m * T + t + 1) * P],
                                                named[name][:, t, c:c + j["d"]], ident[:, :])
                    last.then_inc(*lane.tick(a_full, ("full", "a", n)))

                def scores(i):
                    j = jobs[i]
                    d, keys = j["d"], j.get("keys", S)
                    if "q" in j:
                        pe.wait_ge(*lane.of(("heads", stage_n, i)))
                        qT = QK[0:d, i % 2, 0:2, :].rearrange("p a n -> p (a n)")
                    else:
                        qT = hT[:, j["qT"][1], :]
                    if "k" in j:
                        kT = QK[0:d, i % 2, 2:4, :].rearrange("p a n -> p (a n)")
                    else:
                        kT = cT if j["kT"] == "cT" else KC[:, j["kT"][1], :]
                    b, n = bank(lane, "d")
                    pe.wait_ge(*emptied(lane, "d", n))
                    for t in range(T):
                        last = pe.matmul(b[:, t * keys:(t + 1) * keys], qT[:, t * P:(t + 1) * P], kT,
                                         start=True, stop=True)
                    last.then_inc(*lane.tick(d_full, ("full", "d", n), ("scores", stage_n, i)))

                def turn_probs(i):
                    j = jobs[i]
                    keys = j.get("keys", S)
                    pe.wait_ge(*lane.of(("probs", stage_n, i)))
                    b, n = bank(lane, "a")
                    pe.wait_ge(*emptied(lane, "a", n))
                    for kc in range(-(-keys // P)):
                        w = min(P, keys - kc * P)
                        for t in range(T):
                            last = pe.transpose(b[0:w, (kc * T + t) * P:(kc * T + t + 1) * P],
                                                PR[:, i % 2, t, kc * P:kc * P + w], ident[:, :])
                    last.then_inc(*lane.tick(a_full, ("full", "a", n), ("probs_turned", stage_n, i)))

                def values(i):
                    j = jobs[i]
                    keys, dv = j.get("keys", S), j["dv"]
                    pe.wait_ge(*lane.of(("pt", stage_n, i)))
                    b, n = bank(lane, "x")
                    pe.wait_ge(*emptied(lane, "x", n))
                    chunks = -(-keys // P)
                    for t in range(T):
                        for kc in range(chunks):
                            w = min(P, keys - kc * P)
                            v = VCMP[:, j["v"][1], :] if j["v"][0] == "VCMP" else \
                                named[j["v"][0]][:, kc, j["v"][1]:j["v"][1] + dv]
                            last = pe.matmul(b[:, t * dv:(t + 1) * dv], PT[0:w, i % 2, kc, t, :], v,
                                             start=(kc == 0), stop=(kc == chunks - 1))
                    last.then_inc(*lane.tick(x_full, ("full", "x", n), ("values", stage_n, i)))

                for i in range(count + 4):
                    if i < count:
                        heads(i)
                    if 0 <= i - 1 < count:
                        scores(i - 1)
                    if 0 <= i - 3 < count:
                        turn_probs(i - 3)
                    if 0 <= i - 4 < count:
                        values(i - 4)

            def gate_up(group):
                gv, uv = slot(group["gate"]), slot(group["up"])
                for f0 in range(0, group["w"] // P, 2):
                    for w, v, r in (("gate", gv, "a"), ("up", uv, "d")):
                        b, n = bank(lane, r)
                        pe.wait_ge(*emptied(lane, r, n))
                        for f in range(2):
                            for k in range(KD):
                                last = pe.matmul(b[:, f * S:(f + 1) * S], v[:, k, (f0 + f) * P:(f0 + f + 1) * P],
                                                 hT[:, k, :], start=(k == 0), stop=(k == KD - 1))
                        last.then_inc(*lane.tick(filled[r], ("full", r, n), ("used", group[w])))
                    state["pair"] += 1
                group_pair = state["pair"] - 1
                return group_pair

            def down(group, n_group, pair, accs, first, final):
                v = slot(group["down"])
                nf = group["w"] // P
                for f in range(nf):
                    if f % 2 == 0:
                        pe.wait_ge(*lane.of(("hidden", pair - (nf - 1) // 2 + f // 2)))
                    for t in range(T):
                        for half in range(2):
                            b, n = accs[2 * t + half]
                            start, stop = first and f == 0, final and f == nf - 1
                            last = pe.matmul(b[:, :], hid[:, n_group % 2, f, t * P:(t + 1) * P],
                                             v[:, f, half * 512:(half + 1) * 512], start=start, stop=stop)
                            if stop:
                                last.then_inc(*lane.tick(x_full, ("full", "x", n)))
                if final:
                    lane.mark(("down", n_group), ("used", group["down"]))
                else:
                    last.then_inc(*lane.tick(down_done, ("down", n_group), ("used", group["down"])))

            def ffn(groups):
                late, accs = None, None
                for g, group in enumerate(groups):
                    pair = gate_up(group)
                    n_group = state["group"]
                    state["group"] += 1
                    if late is not None:
                        if accs is None:
                            accs = [bank(lane, "x") for _ in range(4)]
                            for _, n in accs:
                                pe.wait_ge(*emptied(lane, "x", n))
                        down(*late, accs, g == 1, False)
                    late = (group, n_group, pair)
                down(*late, accs, False, True)

            def small_turn(parts, width):
                b, n = bank(lane, "a")
                pe.wait_ge(*emptied(lane, "a", n))
                for m, piece in enumerate(parts):
                    last = pe.transpose(b[0:width, m * P:(m + 1) * P], piece, ident[:, :])
                last.then_inc(*lane.tick(a_full, ("full", "a", n)))

            def index_scores(stage_n):
                for pair in range(4):
                    small_turn([proj[:, t, 640 + HD * h:704 + HD * h] for h in (2 * pair, 2 * pair + 1)
                                for t in range(T)], HD)
                small_turn([proj[:, t, 1152:1216] for t in range(T)], HD)
                pe.wait_ge(*lane.of(("index_turned", stage_n)))
                for h in range(8):
                    b, n = bank(lane, "a")
                    pe.wait_ge(*emptied(lane, "a", n))
                    for t in range(T):
                        last = pe.matmul(b[:, t * S:(t + 1) * S], hT[0:HD, h, t * P:(t + 1) * P],
                                         QK[0:HD, 0, 0:2, :].rearrange("p a n -> p (a n)"), start=True, stop=True)
                    last.then_inc(*lane.tick(a_full, ("full", "a", n)))

            def latent_heads(s, stage_n):
                small_turn([proj[:, t, 512:640] for t in range(T)], P)
                for pair in range(4):
                    small_turn([proj[:, t, HD * h:HD * h + HD] for h in (2 * pair, 2 * pair + 1) for t in range(T)],
                               HD)
                    pe.wait_ge(*lane.of(("latent_turned", pair)))
                    uk = slot(s["uk"])
                    b, n = bank(lane, "a")
                    pe.wait_ge(*emptied(lane, "a", n))
                    for m in range(2):
                        last = pe.matmul(b[:, m * S:(m + 1) * S], uk[:, 2 * pair + m, :],
                                         QK[0:HD, pair % 2, 2 * m:2 * m + 2, :].rearrange("p a n -> p (a n)"),
                                         start=True, stop=True)
                    last.then_inc(*lane.tick(a_full, ("full", "a", n), ("used", s["uk"]), ("latent_scored", pair)))
                uv = slot(s["uv"]).rearrange("p k c -> p (k c)")
                for t in range(T):
                    b, n = bank(lane, "a")
                    pe.wait_ge(*emptied(lane, "a", n))
                    pe.matmul(b[:, :], cT[:, t * P:(t + 1) * P], uv, start=True, stop=True).then_inc(*lane.tick(a_full, ("full", "a", n), ("used", s["uv"])))

            def compress(s, stage_n):
                base = 1024 + P * s["n"]
                small_turn([proj[:, t, base + HD * g:base + HD * g + HD] for g in range(2) for t in range(T)], HD)
                pe.wait_ge(*lane.of(("pe", s["n"])))
                b, n = bank(lane, "a")
                pe.wait_ge(*emptied(lane, "a", n))
                pe.transpose(b[0:HD, 0:32], PEN, ident[0:32, 0:32]).then_inc(*lane.tick(a_full, ("full", "a", n)))
                pe.wait_ge(*lane.of(("blocks", s["n"])))
                w1 = slot(s["w1"])
                b, n = bank(lane, "d")
                pe.wait_ge(*emptied(lane, "d", n))
                for i in range(32):
                    last = pe.matmul(b[:, 0:2 * CMP], w1[:, i, :], KPE[:, :, i, :], start=(i == 0), stop=(i == 31))
                last.then_inc(*lane.tick(d_full, ("full", "d", n), ("used", s["w1"])))
                pe.wait_ge(*lane.of(("gelu", s["n"])))
                w2 = slot(s["w2"])
                b, n = bank(lane, "a")
                pe.wait_ge(*emptied(lane, "a", n))
                if s["n"] == 0:
                    last = pe.matmul(b[0:HD, 0:2 * CMP], w2[:, 0, :], GEL[:, 5, 0:2 * CMP], start=True, stop=True)
                else:
                    for g in range(2):
                        last = pe.matmul(b[0:CMP, g * HD:(g + 1) * HD], GEL[:, 5, g * CMP:(g + 1) * CMP],
                                         w2[:, 0, :], start=True, stop=True)
                last.then_inc(*lane.tick(a_full, ("full", "a", n), ("used", s["w2"])))

            def route():
                pe.wait_ge(*lane.of(("index",)))
                pe.wait_ge(*lane.of(("chosen",)))
                b, n = bank(lane, "d")
                pe.wait_ge(*emptied(lane, "d", n))
                pe.matmul(b[:, 0:8], earlier, chosen[:, 0, :], start=True, stop=True)
                pe.matmul(b[:, 8:16], every, chosen[:, 0, :], start=True, stop=False)
                pe.matmul(b[:, 8:16], earlier, chosen[:, 1, :], start=False, stop=True)
                pe.matmul(b[:, 16:24], every, chosen[:, 0, :], start=True, stop=False)
                pe.matmul(b[:, 16:24], every, chosen[:, 1, :], start=False, stop=True).then_inc(
                    *lane.tick(d_full, ("full", "d", n)))

            def expert(groups):
                m = state["pass"]
                state["pass"] += 1
                pe.wait_ge(*lane.of(("picked", m)))
                for k0 in (0, 4):
                    b, n = bank(lane, "a")
                    pe.wait_ge(*emptied(lane, "a", n))
                    for k in range(k0, k0 + 4):
                        for t in range(T):
                            last = pe.matmul(b[:, (k - k0) * P:(k - k0 + 1) * P], X[:, t, k * P:(k + 1) * P],
                                             pick[:, m % 2, t, :], start=(t == 0), stop=(t == T - 1))
                    last.then_inc(*lane.tick(a_full, ("full", "a", n), ("gathered", m)))
                b, n = bank(lane, "a")
                pe.wait_ge(*emptied(lane, "a", n))
                for t in range(T):
                    last = pe.transpose(b[:, t * P:(t + 1) * P], weigh[:, m % 2, t, :], ident[:, :])
                last.then_inc(*lane.tick(a_full, ("full", "a", n), ("weigh_turned", m)))
                pe.wait_ge(*lane.of(("xg", m)))
                late, accs = None, None
                for g, group in enumerate(groups + [None]):
                    if group:
                        for w, r, full in (("gate", "a", a_full), ("up", "d", d_full)):
                            v = slot(group[w])
                            b, n = bank(lane, r)
                            pe.wait_ge(*emptied(lane, r, n))
                            for f in range(4):
                                for k in range(KD):
                                    last = pe.matmul(b[:, f * P:(f + 1) * P], v[:, k, f * P:(f + 1) * P],
                                                     xg[:, m % 2, k, :], start=(k == 0), stop=(k == KD - 1))
                            last.then_inc(*lane.tick(full, ("full", r, n), ("used", group[w])))
                    if late:
                        if accs is None:
                            accs = [bank(lane, "x") for _ in range(2)]
                            for _, n in accs:
                                pe.wait_ge(*emptied(lane, "x", n))
                        n_group = state["e_group"]
                        state["e_group"] += 1
                        v = slot(late["down"])
                        pe.wait_ge(*lane.of(("e_hidden", n_group)))
                        for f in range(4):
                            for half in range(2):
                                b, n = accs[half]
                                stop = group is None and f == 3
                                last = pe.matmul(b[:, :], hid_e[:, n_group % 2, f, :],
                                                 v[:, f, half * 512:(half + 1) * 512],
                                                 start=(g == 1 and f == 0), stop=stop)
                                if stop:
                                    last.then_inc(*lane.tick(x_full, ("full", "x", n)))
                        if group:
                            last.then_inc(*lane.tick(down_done, ("e_down", n_group), ("used", late["down"])))
                        else:
                            lane.mark(("e_down", n_group), ("used", late["down"]))
                    late = group
                pe.wait_ge(*lane.of(("give", m)))
                pe.wait_ge(*lane.of(("y_e", m)))
                for t in range(T):
                    for half in range(2):
                        b, n = bank(lane, "x")
                        pe.wait_ge(*emptied(lane, "x", n))
                        pe.matmul(b[:, :], give[:, m % 2, t * P:(t + 1) * P], y_e[:, half * 512:(half + 1) * 512],
                                  start=True, stop=True).then_inc(*lane.tick(x_full, ("full", "x", n), ("given", m)))

            for n, (kind, s) in enumerate(stages):
                if kind == "lines":
                    pe.wait_ge(*lane.of(("const",)))
                    b, m = bank(lane, "d")
                    pe.wait_ge(*emptied(lane, "d", m))
                    pe.matmul(b[0:16, :], table, onehot, start=True, stop=True).then_inc(*lane.tick(d_full, ("full", "d", m)))
                elif kind in ("turn", "linear", "attend", "ffn", "index_scores", "latent_heads", "compress", "experts"):
                    pe.wait_ge(*lane.of(("done", "scalar", n - 1)))
                    pe.wait_ge(*lane.of(("done", "vector", n - 1)))
                    pe.wait_ge(*lane.of(("done", "gpsimd", n - 1)))
                if kind == "turn":
                    if s["dst"] == "memT":
                        pe.wait_ge(*lane.of(("mem",)))
                    turn(s)
                elif kind == "linear":
                    linear(s)
                elif kind == "attend":
                    attend(s, n)
                elif kind == "ffn":
                    ffn(s["groups"])
                elif kind == "index_scores":
                    index_scores(n)
                elif kind == "latent_heads":
                    latent_heads(s, n)
                elif kind == "compress":
                    compress(s, n)
                elif kind == "experts":
                    with lane.loop(pe, s["tile"] + 1) as turn:
                        for u, groups in enumerate(s["groups"]):
                            if s["tile"] == 0:
                                expert(groups)
                                continue
                            start, before = dict(lane.count), lane.own()
                            tokens = pe.value_load(loads[0:1, bass.ds(turn * BODY + u, 1)], min_val=0, max_val=S)
                            with pe.If(tokens > P * s["tile"]):
                                expert(groups)
                            with pe.Else():
                                pe.wait_ge(*before)
                                for sem, count in lane.since(start):
                                    pe.sem_inc(sem, count)
                elif kind == "route":
                    route()
                leave(lane, n)

        @block.scalar
        def _(act):
            lane = Lane(book, "scalar", x_landed)
            state = {"pair": 0, "root": 0, "pass": 0, "e_group": 0}

            def root():
                r = state["root"]
                state["root"] += 1
                act.wait_ge(*lane.of(("variance", r)))
                w = book["width"].get(r, 1)
                act.activation(stat[:, 0:w], stat[:, 0:w], ACT.Sqrt).then_inc(*lane.tick(act_order, ("root", r)))

            def turn(s):
                dst = named[s["dst"]]
                for k0 in range(0, s["chunks"], 2):
                    b, n = bank(lane, "a")
                    act.wait_ge(*lane.of(("full", "a", n)))
                    w = min(2, s["chunks"] - k0)
                    act.activation(dst[:, k0:k0 + w, :].rearrange("p k s -> p (k s)"), b[:, 0:w * S], ACT.Copy).then_inc(*lane.tick(a_free, ("free", "a", n)))

            def linear(s):
                dst = named[s["dst"]]
                for _, c0, c in s["blocks"]:
                    for t in range(T):
                        for j in range(0, c, 512):
                            b, n = bank(lane, "a")
                            act.wait_ge(*lane.of(("full", "a", n)))
                            w = min(512, c - j)
                            act.activation(dst[:, t, c0 + j:c0 + j + w], b[:, 0:w], ACT.Copy).then_inc(*lane.tick(a_free, ("free", "a", n)))

            def attend(s, stage_n):
                jobs = s["jobs"]
                count = len(jobs)

                def heads(i):
                    j = jobs[i]
                    if "q" not in j:
                        return
                    b, n = bank(lane, "a")
                    act.wait_ge(*lane.of(("full", "a", n)))
                    if i >= 2:
                        act.wait_ge(*lane.of(("scores", stage_n, i - 2)))
                    w = 4 if "k" in j else 2
                    act.activation(QK[0:j["d"], i % 2, 0:w, :].rearrange("p a n -> p (a n)"),
                                         b[0:j["d"], 0:w * P], ACT.Copy).then_inc(*lane.tick(a_free, ("free", "a", n), ("heads", stage_n, i)))

                def exps(i):
                    j = jobs[i]
                    keys = j.get("keys", S) + ("sink" in j)
                    act.wait_ge(*lane.of(("max", stage_n, i)))
                    if i >= 2:
                        act.wait_ge(*lane.of(("probs_turned", stage_n, i - 2)))
                    if i >= 4:
                        act.wait_ge(*lane.of(("normed", stage_n, i - 4)))
                    for t in range(T):
                        act.activation(PR[:, i % 2, t, 0:keys], SC[:, i % 2, t, 0:keys], ACT.Exp,
                                                   bias=negmax[:, i % 4, t:t + 1], accum_out=total[:, i % 4, t:t + 1]).then_inc(*lane.tick(exped, ("probs", stage_n, i)))

                def turned(i):
                    keys = jobs[i].get("keys", S)
                    b, n = bank(lane, "a")
                    act.wait_ge(*lane.of(("full", "a", n)))
                    if i >= 2:
                        act.wait_ge(*lane.of(("values", stage_n, i - 2)))
                    w = min(P, keys)
                    m = -(-keys // P)
                    act.activation(PT[0:w, i % 2, 0:m].rearrange("p k t n -> p (k t n)"), b[0:w, 0:m * T * P],
                                         ACT.Copy).then_inc(*lane.tick(a_free, ("free", "a", n), ("pt", stage_n, i)))

                for i in range(count + 4):
                    if i < count:
                        heads(i)
                    if 0 <= i - 2 < count:
                        exps(i - 2)
                    if 0 <= i - 3 < count:
                        turned(i - 3)

            def ffn(groups):
                for group in groups:
                    for _ in range(group["w"] // P // 2):
                        b, n = bank(lane, "a")
                        act.wait_ge(*lane.of(("full", "a", n)))
                        p = state["pair"]
                        state["pair"] += 1
                        act.wait_ge(*lane.back(("hidden",), p - 2))
                        act.activation(silu[:, p % 2, :], b[:, :], ACT.Silu).then_inc(*lane.tick(a_free, ("free", "a", n), ("silu", p)))

            def expert(groups):
                m = state["pass"]
                state["pass"] += 1
                for k0 in (0, 4):
                    b, n = bank(lane, "a")
                    act.wait_ge(*lane.of(("full", "a", n)))
                    act.activation(xg[:, m % 2, k0:k0 + 4, :].rearrange("p k s -> p (k s)"), b[:, :], ACT.Copy).then_inc(
                        *lane.tick(a_free, ("free", "a", n), ("xg", m)))
                b, n = bank(lane, "a")
                act.wait_ge(*lane.of(("full", "a", n)))
                act.wait_ge(*lane.back(("given",), m - 2))
                act.activation(give[:, m % 2, :], b[:, 0:S], ACT.Copy).then_inc(
                    *lane.tick(a_free, ("free", "a", n), ("give", m)))
                for _ in groups:
                    b, n = bank(lane, "a")
                    act.wait_ge(*lane.of(("full", "a", n)))
                    g = state["e_group"]
                    state["e_group"] += 1
                    act.wait_ge(*lane.back(("e_hidden",), g - 2))
                    act.activation(silu_e[:, g % 2, :], b[:, :], ACT.Silu).then_inc(
                        *lane.tick(a_free, ("free", "a", n), ("e_silu", g)))

            def plain(dst, w, parts=P, *keys, func=ACT.Copy, scale=1.0):
                b, n = bank(lane, "a")
                act.wait_ge(*lane.of(("full", "a", n)))
                act.activation(dst, b[0:parts, 0:w], func, scale=scale).then_inc(*lane.tick(a_free, ("free", "a", n), *keys))

            for n, (kind, s) in enumerate(stages):
                if kind in ("turn", "linear", "attend", "ffn", "experts", "index_scores", "latent_heads",
                            "compress", "gates", "route", "diff_out"):
                    act.wait_ge(*lane.of(("done", "tensor", n - 1)))
                    act.wait_ge(*lane.of(("done", "vector", n - 1)))
                    act.wait_ge(*lane.of(("done", "gpsimd", n - 1)))
                if kind == "turn":
                    turn(s)
                elif kind == "linear":
                    linear(s)
                elif kind == "attend":
                    attend(s, n)
                elif kind in ("rms_pre", "rms_add", "layer_norm", "latent_norm"):
                    root()
                elif kind == "head_norms":
                    root()
                elif kind == "diff_out":
                    act.wait_ge(*lane.of(("lambda", s["l"])))
                    act.activation(stat[:, 0:2], stat[:, 0:2], ACT.Exp).then_inc(*lane.tick(act_order, ("lambda_exp", s["l"])))
                    root()
                elif kind == "ffn":
                    ffn(s["groups"])
                elif kind == "index_scores":
                    for pair in range(4):
                        plain(hT[0:HD, 2 * pair:2 * pair + 2, :].rearrange("p k s -> p (k s)"), 512, HD)
                    plain(QK[0:HD, 0, 0:2, :].rearrange("p a n -> p (a n)"), S, HD, ("index_turned", n))
                    for h in range(8):
                        if h >= 2:
                            act.wait_ge(*lane.of(("indexed", h - 2)))
                        plain(SC[:, h % 2, :, 0:S], 512, P, ("relu", h), func=ACT.Relu, scale=HD ** -0.5)
                elif kind == "latent_heads":
                    plain(cT, S)
                    for pair in range(4):
                        if pair >= 2:
                            act.wait_ge(*lane.of(("latent_scored", pair - 2)))
                        plain(QK[0:HD, pair % 2, :, :].rearrange("p a n -> p (a n)"), 512, HD, ("latent_turned", pair))
                        plain(hT[:, 2 * pair:2 * pair + 2, :].rearrange("p k s -> p (k s)"), 512)
                    for t in range(T):
                        plain(VC[:, t, :], 512)
                elif kind == "gates":
                    act.wait_ge(*lane.own())
                    act.activation(gate_t[:, :, :], proj[:, :, 1792:1840], ACT.Exp, scale=-1.0).then_inc(*lane.tick(act_order, ("gate_exp",)))
                elif kind == "compress":
                    plain(QK[0:HD, 0, :, :].rearrange("p a n -> p (a n)"), 512, HD)
                    plain(PET, 32, HD, ("compress_turned", s["n"]))
                    act.wait_ge(*lane.of(("gelu_arg", s["n"])))
                    act.activation(GEL[:, 4, 0:2 * CMP], GEL[:, 3, 0:2 * CMP], ACT.Exp,
                                               scale=-2.0 * math.sqrt(2.0 / math.pi)).then_inc(*lane.tick(act_order, ("gelu_exp", s["n"])))
                    if s["n"] == 0:
                        plain(KC.rearrange("p g n -> p (g n)"), 2 * CMP, HD)
                    else:
                        plain(VCMP.rearrange("p g n -> p (g n)"), 2 * HD, CMP)
                elif kind == "route":
                    act.wait_ge(*lane.of(("route_arg",)))
                    act.activation(route[:, 32:34], route[:, 32:34], ACT.Exp).then_inc(*lane.tick(act_order, ("route_exp",)))
                elif kind == "experts":
                    with lane.loop(act, s["tile"] + 1) as turn:
                        for u, groups in enumerate(s["groups"]):
                            if s["tile"] == 0:
                                expert(groups)
                                continue
                            start, before = dict(lane.count), lane.own()
                            tokens = act.value_load(loads[0:1, bass.ds(turn * BODY + u, 1)], min_val=0, max_val=S)
                            with act.If(tokens > P * s["tile"]):
                                expert(groups)
                            with act.Else():
                                act.wait_ge(*before)
                                for sem, count in lane.since(start):
                                    act.sem_inc(sem, count)
                leave(lane, n)

        @block.vector
        def _(dve):
            lane = Lane(book, "vector", x_landed)
            state = {"pair": 0, "root": 0, "group": 0, "pass": 0, "e_group": 0}

            def do(ins, *keys, sem=dve_order):
                ins.then_inc(*lane.tick(sem, *keys))
                dve.wait_ge(*lane.own())

            def post(ins, *keys, sem=dve_order):
                ins.then_inc(*lane.tick(sem, *keys))

            def inv_root(width, source, scale, eps):
                r = state["root"]
                state["root"] += 1
                book["width"][r] = width
                do(dve.tensor_scalar(stat[:, 0:width], source, scale, eps, ALU.mult, ALU.add), ("variance", r))
                dve.wait_ge(*lane.of(("root", r)))
                do(dve.reciprocal(stat[:, 0:width], stat[:, 0:width]))

            def squares(src, width, scratch):
                for t in range(T):
                    do(dve.tensor_tensor_reduce(scratch[:, t, 0:width], src[:, t, :], src[:, t, :], 1.0, 0.0,
                                                ALU.mult, ALU.add, stat[:, 32 + t:33 + t]))

            def use_vec(m):
                dve.wait_ge(*lane.of(("vec", m)))
                return vec[:, m % VEC_SLOTS, :]

            def rms_pre(s):
                squares(X, D, N)
                inv_root(T, stat[:, 32:34], 1.0 / D, EPS)
                w = use_vec(s["vec"])
                for t in range(T):
                    post(dve.scalar_tensor_tensor(N[:, t, :], X[:, t, :], stat[:, t:t + 1], w, ALU.mult, ALU.mult),
                         ("vec_used", s["vec"]))

            def rms_add(s):
                squares(N, D, O)
                inv_root(T, stat[:, 32:34], 1.0 / D, EPS)
                w = use_vec(s["vec"])
                for t in range(T):
                    do(dve.scalar_tensor_tensor(N[:, t, :], N[:, t, :], stat[:, t:t + 1], w, ALU.mult, ALU.mult),
                       ("vec_used", s["vec"]))
                    do(dve.tensor_tensor(X[:, t, :], X[:, t, :], N[:, t, :], ALU.add))

            def layer_norm(s):
                g, b = use_vec(s["gain"]), use_vec(s["shift"])
                for t in range(T):
                    do(dve.scalar_tensor_tensor(X[:, t, :], X[:, t, :], ALPHA, N[:, t, :], ALU.mult, ALU.add))
                    for c in range(2):
                        do(dve.bn_stats(stat[:, 36 + 6 * c:42 + 6 * c], X[:, t, 512 * c:512 * c + 512]))
                    do(dve.bn_aggr(stat[:, 32 + 2 * t:34 + 2 * t], stat[:, 36:48]))
                inv_root(T, stat[:, 33:36:2], 1.0, LN_EPS)
                for t in range(T):
                    do(dve.tensor_scalar(X[:, t, :], X[:, t, :], stat[:, 32 + 2 * t:33 + 2 * t], stat[:, t:t + 1],
                                         ALU.subtract, ALU.mult))
                    do(dve.tensor_tensor(X[:, t, :], X[:, t, :], g, ALU.mult), ("vec_used", s["gain"]))
                    do(dve.tensor_tensor(X[:, t, :], X[:, t, :], b, ALU.add), ("vec_used", s["shift"]))

            def rope(x, cos, sin):
                shape = [P, x.shape[1], x.shape[2], 16]
                size = shape[1] * shape[2] * 16
                x1, x2 = x[:, :, :, 0, :], x[:, :, :, 1, :]
                c, s = cos.unsqueeze(1).broadcast_to(shape), sin.unsqueeze(1).broadcast_to(shape)
                tmp = [SC[:, m // 2, m % 2, 0:size].rearrange("p (h b c) -> p h b c", h=shape[1], b=shape[2])
                       for m in range(4)]
                for m, (u, v) in enumerate(((x1, c), (x2, s), (x2, c), (x1, s))):
                    do(dve.tensor_tensor(tmp[m], u, v, ALU.mult))
                do(dve.tensor_tensor(x1, tmp[0], tmp[1], ALU.subtract))
                do(dve.tensor_tensor(x2, tmp[2], tmp[3], ALU.add))

            def head_norms(s):
                dve.wait_ge(*lane.of(("small", s["l"])))
                gq = proj[:, :, GQ_Q:GQ_V].rearrange("p t (h c) -> p t h c", h=6)
                for t in range(T):
                    sq = PR[:, t, :, 0:192].rearrange("p a c -> p a c")
                    x = proj[:, t, GQ_Q:GQ_V].rearrange("p (a c) -> p a c", a=2)
                    do(dve.tensor_tensor(sq, x, x, ALU.mult))
                    for half in range(2):
                        do(dve.tensor_reduce(stat[:, 32 + 6 * t + 3 * half:35 + 6 * t + 3 * half],
                                             PR[:, t, half, 0:192].rearrange("p (h c) -> p h c", h=3), AX, ALU.add))
                    for n, (c0, w) in enumerate(((ML_Q, 256), (ML_KV, 128))):
                        x = proj[:, t, c0:c0 + w]
                        do(dve.tensor_tensor_reduce(PR[:, t, 0, 0:w], x, x, 64.0 / w, 0.0, ALU.mult, ALU.add,
                                                    stat[:, 44 + 2 * t + n:45 + 2 * t + n]))
                inv_root(16, stat[:, 32:48], 1.0 / HD, EPS)
                for t in range(T):
                    x = gq[:, t]
                    do(dve.tensor_tensor(x, x, stat[:, 6 * t:6 * t + 6].unsqueeze(2).broadcast_to([P, 6, HD]), ALU.mult))
                    for h0, h1, at in ((0, 4, SV_GQ), (4, 6, SV_GK)):
                        w = small[:, at:at + HD].unsqueeze(1).broadcast_to([P, h1 - h0, HD])
                        do(dve.tensor_tensor(x[:, h0:h1, :], x[:, h0:h1, :], w, ALU.mult))
                    for n, (c0, w, at) in enumerate(((ML_Q, 256, SV_MQ), (ML_KV, 128, SV_MKV))):
                        x = proj[:, t, c0:c0 + w]
                        do(dve.scalar_tensor_tensor(x, x, stat[:, 12 + 2 * t + n:13 + 2 * t + n], small[:, at:at + w],
                                                    ALU.mult, ALU.mult))
                    rope(proj[:, t, GQ_Q:GQ_V].rearrange("p (h b a c) -> p h b a c", h=6, b=2, a=2),
                         rope_t[:, t, 0:2, 0, :], rope_t[:, t, 0:2, 1, :])

            def mla_keys():
                for t in range(T):
                    kr = proj[:, t, ML_KR:ML_KR + 32].rearrange("p (h b a c) -> p h b a c", h=1, b=1, a=2)
                    cos, sin = rope_t[:, t, 2:3, 0, :], rope_t[:, t, 2:3, 1, :]
                    rope(kr, cos, sin)
                    q = QF[:, t, :].rearrange("p (h c) -> p h c", h=4)[:, :, 64:96]
                    rope(q.unsqueeze(2).rearrange("p h b (a c) -> p h b a c", a=2), cos, sin)
                    k = KF[:, t, :].rearrange("p (h c) -> p h c", h=4)
                    do(dve.tensor_copy(k[:, :, 0:64], KV[:, t, :].rearrange("p (h c) -> p h c", h=4)[:, :, 0:64]))
                    do(dve.tensor_copy(k[:, :, 64:96], proj[:, t, ML_KR:ML_KR + 32].unsqueeze(1).broadcast_to(
                        [P, 4, 32])))

            def attend(s, stage_n):
                jobs = s["jobs"]
                count = len(jobs)

                def scores(i):
                    j = jobs[i]
                    keys = j.get("keys", S)
                    b, n = bank(lane, "d")
                    dve.wait_ge(*lane.of(("full", "d", n)))
                    if i >= 2:
                        dve.wait_ge(*lane.of(("probs", stage_n, i - 2)))
                    got = b[:, 0:T * keys].rearrange("p (t k) -> p t k", t=T)
                    sc = SC[:, i % 2, :, 0:keys]
                    if j["bias"] is None:
                        do(dve.tensor_scalar(sc, got, j["scale"], None, ALU.mult), ("free", "d", n), sem=d_free)
                    else:
                        dve.wait_ge(*lane.of(("bias", j["bias"])))
                        tile = bias_t[:, j["bias"] % BIAS_SLOTS]
                        if j.get("selected"):
                            do(dve.tensor_tensor(tile, tile, score, ALU.add))
                        if keys != S:
                            tile = tile[:, :, 31:31 + 16 * (CMP - 1) + 1:16]
                        do(dve.scalar_tensor_tensor(sc, got, j["scale"], tile, ALU.mult, ALU.add),
                           ("free", "d", n), *([("bias_used", j["bias"])] if j["bias_last"] else []), sem=d_free)
                    width = keys
                    if "sink" in j:
                        width += 1
                        do(dve.tensor_copy(SC[:, i % 2, :, keys:keys + 1],
                                           small[:, P + j["sink"]:P + j["sink"] + 1].unsqueeze(1).broadcast_to(
                                               [P, T, 1])))
                    nm = negmax[:, i % 4, :]
                    last = dve.tensor_reduce(nm, SC[:, i % 2, :, 0:width], AX, ALU.max, negate=True)
                    if keys != S:
                        do(last)
                        last = dve.tensor_scalar(nm, nm, 1e20, None, ALU.min)
                    post(last, ("max", stage_n, i), sem=maxed)

                def normed(i):
                    j = jobs[i]
                    dv = j["dv"]
                    dve.wait_ge(*lane.of(("probs", stage_n, i)))
                    r = inv[:, i % 4, :]
                    if j.get("keys", S) != S:
                        do(dve.tensor_scalar(total[:, i % 4, :], total[:, i % 4, :], 1e-30, None, ALU.add))
                    do(dve.reciprocal(r, total[:, i % 4, :]))
                    if "gate" in j:
                        do(dve.tensor_tensor(r, r, gate_t[:, :, j["gate"]], ALU.mult))
                    b, n = bank(lane, "x")
                    dve.wait_ge(*lane.of(("full", "x", n)))
                    dst = named[j["out"][0]]
                    at = j["out"][1]
                    for t in range(T):
                        o = dst[:, t, at:at + dv] if j["out"][0] != "DO" else DO[:, t, at:at + dv]
                        if j.get("add"):
                            ins = dve.scalar_tensor_tensor(o, b[:, t * dv:(t + 1) * dv], r[:, t:t + 1], o,
                                                           ALU.mult, ALU.add)
                        else:
                            ins = dve.tensor_scalar(o, b[:, t * dv:(t + 1) * dv], r[:, t:t + 1], None, ALU.mult)
                        if t < T - 1:
                            post(ins)
                        else:
                            post(ins, ("free", "x", n), ("normed", stage_n, i), sem=x_free)

                for i in range(count + 4):
                    if 0 <= i - 1 < count:
                        scores(i - 1)
                    if 0 <= i - 4 < count:
                        normed(i - 4)

            def diff_out(s, stage_n):
                l = s["l"]
                init = 0.8 - 0.6 * math.exp(-0.3 * l)
                lam = small[:, SV_LAM:SV_LAM + 128].rearrange("p (a b c) -> p a b c", a=2, b=2)
                for m in range(2):
                    do(dve.tensor_tensor_reduce(PR[:, 0, 0, 0:32], lam[:, m, 0, :], lam[:, m, 1, :], 1.0, 0.0,
                                                ALU.mult, ALU.add, stat[:, m:m + 1]), ("lambda", l))
                dve.wait_ge(*lane.of(("lambda_exp", l)))
                do(dve.tensor_tensor(stat[:, 60:61], stat[:, 1:2], stat[:, 0:1], ALU.subtract))
                do(dve.tensor_scalar(stat[:, 60:61], stat[:, 60:61], -init, None, ALU.add))
                for t in range(T):
                    o = DO[:, t, 0:256]
                    do(dve.scalar_tensor_tensor(o, DO[:, t, 256:512], stat[:, 60:61], o, ALU.mult, ALU.add))
                    do(dve.tensor_tensor(PR[:, 0, t, 0:256], o, o, ALU.mult))
                    do(dve.tensor_reduce(stat[:, 32 + 4 * t:36 + 4 * t],
                                         PR[:, 0, t, 0:256].rearrange("p (h c) -> p h c", h=4), AX, ALU.add))
                inv_root(8, stat[:, 32:40], 1.0 / HD, EPS)
                do(dve.tensor_scalar(small[:, SV_SUB:SV_SUB + HD], small[:, SV_SUB:SV_SUB + HD], 1.0 - init, None,
                                     ALU.mult))
                for t in range(T):
                    o = DO[:, t, 0:256].rearrange("p (h c) -> p h c", h=4)
                    do(dve.tensor_tensor(o, o, stat[:, 4 * t:4 * t + 4].unsqueeze(2).broadcast_to([P, 4, HD]), ALU.mult))
                    do(dve.tensor_tensor(O[:, t, 256:512].rearrange("p (h c) -> p h c", h=4), o,
                                         small[:, SV_SUB:SV_SUB + HD].unsqueeze(1).broadcast_to([P, 4, HD]),
                                         ALU.mult), ("diff", l))

            def select(s):
                dve.wait_ge(*lane.of(("bias", s["bias"])))
                do(dve.tensor_tensor(score, score, bias_t[:, s["bias"] % BIAS_SLOTS], ALU.add),
                   ("bias_used", s["bias"]))
                ones = SC[:, 1, 0, 0:S]
                do(dve.memset(ones, 1.0))
                for t in range(T):
                    do(dve.tensor_copy(work[:, t, :], score[:, t, :]))
                    for r in range(TOPK // 8):
                        do(dve.max(stat[:, 8:16], work[:, t, :]))
                        if r < TOPK // 8 - 1:
                            do(dve.match_replace(work[:, t, :], stat[:, 8:16], work[:, t, :], -3e38))
                    above, equal, order = SC[:, 0, 0, 0:S], SC[:, 0, 1, 0:S], PR[:, 0, 0, 0:S]
                    do(dve.tensor_scalar(above, score[:, t, :], stat[:, 15:16], 0.0, ALU.is_gt, ALU.add,
                                         accum_out=stat[:, 16:17]))
                    do(dve.tensor_scalar(stat[:, 17:18], stat[:, 16:17], -1.0, float(TOPK), ALU.mult, ALU.add))
                    do(dve.tensor_scalar(equal, score[:, t, :], stat[:, 15:16], None, ALU.is_equal))
                    do(dve.tensor_tensor_scan(order, ones, equal, 0.0, ALU.mult, ALU.add))
                    do(dve.scalar_tensor_tensor(order, order, stat[:, 17:18], equal, ALU.is_le, ALU.mult))
                    do(dve.tensor_tensor(order, order, above, ALU.add))
                    do(dve.tensor_scalar(score[:, t, :], order, -1.0, -NEG, ALU.add, ALU.mult))

            def compress(s):
                dve.wait_ge(*lane.of(("compress_turned", s["n"])))
                kt = QK[0:HD, 0, :, :].rearrange("p (g t) n -> p g (t n)", g=2)
                for g in range(2):
                    src = bass.AP(QK, kt[:, g, :].offset, [[kt.ap[0][0], HD], [1, 32], [16, CMP]])
                    do(dve.tensor_tensor(KPE[:, g], src, PET.unsqueeze(2).broadcast_to([HD, 32, CMP]), ALU.add),
                       ("blocks", s["n"]))
                b, n = bank(lane, "d")
                dve.wait_ge(*lane.of(("full", "d", n)))
                w = 2 * CMP
                x, u = GEL[:, 0, 0:w], GEL[:, 1, 0:w]
                do(dve.tensor_copy(x, b[:, 0:w]), ("free", "d", n), sem=d_free)
                do(dve.tensor_tensor(u, x, x, ALU.mult))
                do(dve.tensor_scalar(u, u, 0.044715, 1.0, ALU.mult, ALU.add))
                do(dve.tensor_tensor(GEL[:, 3, 0:w], u, x, ALU.mult), ("gelu_arg", s["n"]))
                dve.wait_ge(*lane.of(("gelu_exp", s["n"])))
                do(dve.tensor_scalar(u, GEL[:, 4, 0:w], 1.0, None, ALU.add))
                do(dve.reciprocal(u, u))
                do(dve.tensor_tensor(GEL[:, 5, 0:w], x, u, ALU.mult), ("gelu", s["n"]))

            def route_tokens():
                dve.wait_ge(*lane.of(("index",)))
                top = route[:, 0:16].rearrange("p (t e) -> p t e", t=T)
                where = route[:, 16:32].bitcast(U32).rearrange("p (t e) -> p t e", t=T)
                for t in range(T):
                    do(dve.max(top[:, t, :], logits[:, t, :]))
                    do(dve.max_index(where[:, t, :], top[:, t, :], logits[:, t, :]))
                    do(dve.tensor_tensor(route[:, 32 + t:33 + t], top[:, t, 1:2], top[:, t, 0:1], ALU.subtract),
                       ("route_arg",))
                dve.wait_ge(*lane.of(("route_exp",)))
                do(dve.tensor_scalar(route[:, 34:36], route[:, 32:34], 1.0, None, ALU.add))
                do(dve.reciprocal(route[:, 34:36], route[:, 34:36]))
                do(dve.tensor_tensor(route[:, 36:38], route[:, 32:34], route[:, 34:36], ALU.mult))
                do(dve.tensor_copy(route[:, 40:56].rearrange("p (t e) -> p t e", t=T), where))
                at = route[:, 40:56].rearrange("p (t e) -> p t e", t=T)
                for t in range(T):
                    do(dve.tensor_scalar(gate_t[:, t, 0:8], small[:, 0:8], at[:, t, 0:1], route[:, 34 + t:35 + t],
                                         ALU.is_equal, ALU.mult))
                    do(dve.tensor_scalar(route[:, 56:64], small[:, 0:8], at[:, t, 1:2], route[:, 36 + t:37 + t],
                                         ALU.is_equal, ALU.mult))
                    do(dve.tensor_tensor(gate_t[:, t, 0:8], gate_t[:, t, 0:8], route[:, 56:64], ALU.add))
                    do(dve.tensor_scalar(chosen[:, t, :], small[:, 0:8], at[:, t, 0:1], None, ALU.is_equal))
                    do(dve.tensor_scalar(route[:, 56:64], small[:, 0:8], at[:, t, 1:2], None, ALU.is_equal))
                    do(dve.tensor_tensor(chosen[:, t, :], chosen[:, t, :], route[:, 56:64], ALU.add))
                do(dve.memset(every, 1.0), ("chosen",))
                do(dve.memset(O[:, :, :], 0.0))
                b, n = bank(lane, "d")
                dve.wait_ge(*lane.of(("full", "d", n)))
                do(dve.tensor_scalar(place, chosen, 1024.0, -1024.0, ALU.mult, ALU.add))
                do(dve.tensor_tensor(place, place, b[:, 0:16].rearrange("p (t e) -> p t e", t=T), ALU.add))
                do(dve.tensor_copy(loads[:, :], b[:, 16:24]), ("free", "d", n), ("loads", 0), sem=d_free)

            def expert(groups, tile, e):
                m = state["pass"]
                state["pass"] += 1
                dve.wait_ge(*lane.back(("gathered",), m - 2))
                dve.wait_ge(*lane.back(("weigh_turned",), m - 2))
                for t in range(T):
                    at = place[:, t, bass.ds(e, 1)]
                    if tile:
                        do(dve.tensor_scalar(pick[:, m % 2, t, :], slot_row, float(P * tile), at, ALU.add,
                                             ALU.is_equal))
                    else:
                        do(dve.tensor_scalar(pick[:, m % 2, t, :], slot_row, at, None, ALU.is_equal))
                    do(dve.tensor_scalar(weigh[:, m % 2, t, :], pick[:, m % 2, t, :], gate_t[:, t, bass.ds(e, 1)],
                                         None, ALU.mult), ("picked", m))
                for _ in groups:
                    g = state["e_group"]
                    state["e_group"] += 1
                    dve.wait_ge(*lane.back(("e_down",), g - 2))
                    dve.wait_ge(*lane.of(("e_silu", g)))
                    b, n = bank(lane, "d")
                    dve.wait_ge(*lane.of(("full", "d", n)))
                    dve.tensor_tensor(hid_e[:, g % 2, :, :].rearrange("p f s -> p (f s)"), silu_e[:, g % 2, :],
                                      b[:, :], ALU.mult).then_inc(
                        *lane.tick(d_free, ("free", "d", n), ("e_hidden", g)))
                for half in range(2):
                    b, n = bank(lane, "x")
                    dve.wait_ge(*lane.of(("full", "x", n)))
                    dve.tensor_copy(y_e[:, half * 512:(half + 1) * 512], b[:, :]).then_inc(
                        *lane.tick(x_free, ("free", "x", n), ("y_e", m)))
                for t in range(T):
                    for half in range(2):
                        b, n = bank(lane, "x")
                        dve.wait_ge(*lane.of(("full", "x", n)))
                        y = O[:, t, 512 * half:512 * half + 512]
                        dve.tensor_tensor(y, y, b[:, :], ALU.add).then_inc(
                            *lane.tick(x_free, ("free", "x", n)))

            def ffn(groups):
                for group in groups:
                    n_group = state["group"]
                    state["group"] += 1
                    dve.wait_ge(*lane.back(("down",), n_group - 2))
                    for f0 in range(0, group["w"] // P, 2):
                        p = state["pair"]
                        state["pair"] += 1
                        dve.wait_ge(*lane.of(("silu", p)))
                        b, n = bank(lane, "d")
                        dve.wait_ge(*lane.of(("full", "d", n)))
                        dve.tensor_tensor(
                            hid[:, n_group % 2, f0:f0 + 2, :].rearrange("p f s -> p (f s)"), silu[:, p % 2, :],
                            b[:, :], ALU.mult).then_inc(*lane.tick(d_free, ("free", "d", n), ("hidden", p)))

            for n, (kind, s) in enumerate(stages):
                if kind not in ("turn", "linear", "load_x", "load_mem", "small", "lines"):
                    dve.wait_ge(*lane.of(("done", "tensor", n - 1)))
                    dve.wait_ge(*lane.of(("done", "scalar", n - 1)))
                    dve.wait_ge(*lane.of(("done", "gpsimd", n - 1)))
                if kind == "lines":
                    dve.wait_ge(*lane.of(("x",)))
                    b, m = bank(lane, "d")
                    dve.wait_ge(*lane.of(("full", "d", m)))
                    for v in range(2):
                        do(dve.tensor_tensor(lines[:, v, :], b[0:16, :], line_mask[:, v, :], ALU.add),
                           ("lines",), ("free", "d", m), sem=d_free)
                    dve.wait_ge(*lane.of(("const",)))
                    dve.wait_ge(*lane.of(("line_stored",)))
                    dve.wait_ge(*lane.of(("table_stored", DEPTH - 1)))
                elif kind == "rms_pre":
                    rms_pre(s)
                elif kind == "rms_add":
                    rms_add(s)
                elif kind == "layer_norm":
                    layer_norm(s)
                elif kind == "head_norms":
                    head_norms(s)
                elif kind == "mla_keys":
                    mla_keys()
                elif kind == "attend":
                    attend(s, n)
                elif kind == "diff_out":
                    diff_out(s, n)
                elif kind == "latent_norm":
                    dve.wait_ge(*lane.of(("latent",)))
                    c = proj[:, :, 512:640]
                    squares(c, P, PR[:, 0, :, :])
                    inv_root(T, stat[:, 32:34], 1.0 / P, LN_EPS)
                    for t in range(T):
                        do(dve.scalar_tensor_tensor(c[:, t, :], c[:, t, :], stat[:, t:t + 1], small[:, 0:P],
                                                    ALU.mult, ALU.mult))
                    do(dve.tensor_scalar(proj[:, :, 1216:1224], proj[:, :, 1216:1224], 8 ** -0.5, None, ALU.mult))
                elif kind == "index_scores":
                    do(dve.memset(score, 0.0))
                    for h in range(8):
                        dve.wait_ge(*lane.of(("relu", h)))
                        for t in range(T):
                            do(dve.scalar_tensor_tensor(score[:, t, :], SC[:, h % 2, t, 0:S],
                                                        proj[:, t, 1216 + h:1217 + h], score[:, t, :],
                                                        ALU.mult, ALU.add), ("indexed", h))
                elif kind == "select":
                    select(s)
                elif kind == "gates":
                    dve.wait_ge(*lane.of(("gate_exp",)))
                    do(dve.tensor_scalar(gate_t[:, :, :], gate_t[:, :, :], 1.0, None, ALU.add))
                    do(dve.reciprocal(gate_t[:, :, :], gate_t[:, :, :]))
                elif kind == "compress":
                    compress(s)
                elif kind == "route":
                    route_tokens()
                elif kind == "ffn":
                    ffn(s["groups"])
                    for t in range(T):
                        for half in range(2):
                            b, m = bank(lane, "x")
                            dve.wait_ge(*lane.of(("full", "x", m)))
                            dve.tensor_copy(N[:, t, 512 * half:512 * half + 512], b[:, :]).then_inc(*lane.tick(x_free, ("free", "x", m)))
                    dve.wait_ge(*lane.own())
                elif kind == "experts":
                    with lane.loop(dve, s["tile"] + 1) as turn:
                        for u, groups in enumerate(s["groups"]):
                            if s["tile"] == 0:
                                expert(groups, s["tile"], turn * BODY + u)
                                continue
                            start, before = dict(lane.count), lane.own()
                            tokens = dve.value_load(loads[0:1, bass.ds(turn * BODY + u, 1)], min_val=0, max_val=S)
                            with dve.If(tokens > P * s["tile"]):
                                expert(groups, s["tile"], turn * BODY + u)
                            with dve.Else():
                                dve.wait_ge(*before)
                                for sem, count in lane.since(start):
                                    dve.sem_inc(sem, count)
                    if s["tile"] == T - 1:
                        do(dve.tensor_copy(N[:, :, :], O[:, :, :]))
                leave(lane, n)


def new_book(old=None):
    old = old or {}
    return {"first": not old, "known": old.get("new", {}), "new": {}, "step": old.get("step_new", {}), "step_new": {},
            "span": old.get("span_new", {}), "span_new": {}, "width": old.get("width", {})}


def kernel(**inputs):
    import numpy as _np
    import concourse.bacc as _bacc
    from concourse import mybir as _mybir
    from concourse.bass_utils import run_bass_kernel_spmd as _run

    host = {k: _np.ascontiguousarray(v) for k, v in inputs.items()}
    host.update(shape_constants())
    book = None
    for _ in range(2):
        book = new_book(book)
        nc = _bacc.Bacc("TRN2", target_bir_lowering=False, num_devices=1)
        a = {k: nc.dram_tensor(f"in_{k}", v.shape, _mybir.dt.from_np(v.dtype), kind="ExternalInput").ap()
             for k, v in host.items()}
        out = nc.dram_tensor("out_0", (1, S, D), F32, kind="ExternalOutput").ap()
        build(nc, a, out, book)
    r = _run(nc, [{f"in_{k}": v for k, v in host.items()}], core_ids=[0])
    return r.results[0]["out_0"]
```
